# Optimizing a Trainium2 kernel written in Bass

```python
import jax, jax.numpy as jnp
from jax import lax
import numpy as np

D_MODEL = 2048
BATCH = 1
SEQ = 256
DEPTH = 1

CHUNK = 64
HEAD_DIM = 64
A_Q_HEADS = D_MODEL // 2 // HEAD_DIM
A_KV_HEADS = A_Q_HEADS // 8
A_GROUP = A_Q_HEADS // A_KV_HEADS
A_WINDOW = 128
A_WINDOW_CHUNKS = A_WINDOW // CHUNK
B_HEADS = D_MODEL // 2 // HEAD_DIM
B_LEFT_CHUNKS = 8
B_REL_CLIP = 256
T5_BUCKETS = 32
T5_MAX_DIST = 128
D_FF = -(-8 * D_MODEL // (3 * 256)) * 256
A_QW = A_Q_HEADS * HEAD_DIM
A_KVW = A_KV_HEADS * HEAD_DIM
B_W = B_HEADS * HEAD_DIM
IN_COLS = A_QW + 2 * A_KVW + 3 * B_W + 2 * D_MODEL
EPS = 1e-6
NEG = -1e30

kernel_name = 'hybrid_swa_sink_chunk_relbias_block'

def rms_norm(x, g):
    xf = x.astype(jnp.float32)
    y = xf * lax.rsqrt(jnp.mean(xf * xf, axis=-1, keepdims=True) + EPS)
    return (y * g.astype(jnp.float32)).astype(x.dtype)

def chunk_band(t, n_left):
    nc = t.shape[1]
    pad = [(0, 0)] * t.ndim
    pad[1] = (n_left, 0)
    tp = jnp.pad(t, pad)
    return jnp.concatenate([tp[:, s:s + nc] for s in range(n_left + 1)], axis=2)

def band_valid(n_chunks, n_left):
    c = jnp.arange(n_chunks)[:, None]
    j = jnp.arange((n_left + 1) * CHUNK)[None, :]
    return (c - n_left) * CHUNK + j >= 0

def band_rel(n_left):
    i = np.arange(CHUNK)[:, None]
    j = np.arange((n_left + 1) * CHUNK)[None, :]
    return j - n_left * CHUNK - i

def t5_bucket(rel):
    nb = T5_BUCKETS // 2
    max_exact = nb // 2
    ret = (rel > 0).astype(np.int32) * nb
    n = np.abs(rel)
    large = max_exact + (np.log(np.maximum(n, 1) / max_exact) / np.log(T5_MAX_DIST / max_exact) * (nb - max_exact)).astype(np.int32)
    large = np.minimum(large, nb - 1)
    return (ret + np.where(n < max_exact, n, large)).astype(np.int32)

def mixer_a(q, k, v, q_g, k_g, sink, t5_bias):
    b, s, _ = q.shape
    nc = s // CHUNK
    n_left = A_WINDOW_CHUNKS - 1
    q = rms_norm(q.reshape(b, s, A_Q_HEADS, HEAD_DIM), q_g).reshape(b, nc, CHUNK, A_KV_HEADS, A_GROUP, HEAD_DIM)
    k = rms_norm(k.reshape(b, s, A_KV_HEADS, HEAD_DIM), k_g).reshape(b, nc, CHUNK, A_KV_HEADS, HEAD_DIM)
    v = v.reshape(b, nc, CHUNK, A_KV_HEADS, HEAD_DIM)
    k_band = chunk_band(k, n_left)
    v_band = chunk_band(v, n_left)
    logits = jnp.einsum('bcqhgd,bckhd->bhgcqk', q, k_band).astype(jnp.float32) * HEAD_DIM ** -0.5
    bucket = t5_bucket(band_rel(n_left))
    bias = t5_bias.astype(jnp.float32)[bucket]
    bias = jnp.transpose(bias, (2, 0, 1)).reshape(A_KV_HEADS, A_GROUP, 1, CHUNK, -1)
    valid = band_valid(nc, n_left)[:, None, :]
    logits = jnp.where(valid, logits + bias, NEG)
    sink_logit = jnp.broadcast_to(sink.astype(jnp.float32).reshape(A_KV_HEADS, A_GROUP, 1, 1, 1), logits.shape[:-1] + (1,))
    probs = jax.nn.softmax(jnp.concatenate([logits, sink_logit], axis=-1), axis=-1)[..., :-1]
    o = jnp.einsum('bhgcqk,bckhd->bcqhgd', probs.astype(v_band.dtype), v_band)
    return o.reshape(b, s, A_QW)

def mixer_b(q, k, v, q_g, k_g, rel_bias):
    b, s, _ = q.shape
    nc = s // CHUNK
    n_left = B_LEFT_CHUNKS
    q = rms_norm(q.reshape(b, s, B_HEADS, HEAD_DIM), q_g).reshape(b, nc, CHUNK, B_HEADS, HEAD_DIM)
    k = rms_norm(k.reshape(b, s, B_HEADS, HEAD_DIM), k_g).reshape(b, nc, CHUNK, B_HEADS, HEAD_DIM)
    v = v.reshape(b, nc, CHUNK, B_HEADS, HEAD_DIM)
    k_band = chunk_band(k, n_left)
    v_band = chunk_band(v, n_left)
    logits = jnp.einsum('bcqhd,bckhd->bhcqk', q, k_band).astype(jnp.float32) * HEAD_DIM ** -0.5
    idx = np.clip(band_rel(n_left), -B_REL_CLIP, B_REL_CLIP) + B_REL_CLIP
    bias = rel_bias.astype(jnp.float32)[:, idx][:, None]
    valid = band_valid(nc, n_left)[:, None, :]
    logits = jnp.where(valid, logits + bias, NEG)
    probs = jax.nn.softmax(logits, axis=-1)
    o = jnp.einsum('bhcqk,bckhd->bcqhd', probs.astype(v_band.dtype), v_band)
    return o.reshape(b, s, B_W)

def setup_inputs(seed: int = 0) -> dict:
    key = jax.random.key(seed)
    ks = jax.random.split(key, 17)

    def nrm(k, shape, scale):
        return jax.random.normal(k, shape, jnp.float32) * scale

    return {
        'x': nrm(ks[0], (BATCH, SEQ, D_MODEL), 1.0),
        'norm_mix_g': 1.0 + nrm(ks[1], (DEPTH, D_MODEL), 0.02),
        'w_in': nrm(ks[2], (DEPTH, D_MODEL, IN_COLS), D_MODEL ** -0.5),
        'q_norm_a': 1.0 + nrm(ks[3], (DEPTH, HEAD_DIM), 0.02),
        'k_norm_a': 1.0 + nrm(ks[4], (DEPTH, HEAD_DIM), 0.02),
        'sink_a': nrm(ks[5], (DEPTH, A_Q_HEADS), 1.0),
        't5_bias': nrm(ks[6], (T5_BUCKETS, A_Q_HEADS), 0.3),
        'q_norm_b': 1.0 + nrm(ks[7], (DEPTH, HEAD_DIM), 0.02),
        'k_norm_b': 1.0 + nrm(ks[8], (DEPTH, HEAD_DIM), 0.02),
        'rel_bias_b': nrm(ks[9], (DEPTH, B_HEADS, 2 * B_REL_CLIP + 1), 0.3),
        'w_branch_a': nrm(ks[10], (DEPTH, A_QW, D_MODEL), A_QW ** -0.5),
        'w_branch_b': nrm(ks[11], (DEPTH, B_W, D_MODEL), B_W ** -0.5),
        'w_out': nrm(ks[12], (DEPTH, D_MODEL, D_MODEL), D_MODEL ** -0.5),
        'norm_ffn_g': 1.0 + nrm(ks[13], (DEPTH, D_MODEL), 0.02),
        'w_ffn_gate': nrm(ks[14], (DEPTH, D_MODEL, D_FF), D_MODEL ** -0.5),
        'w_ffn_up': nrm(ks[15], (DEPTH, D_MODEL, D_FF), D_MODEL ** -0.5),
        'w_ffn_down': nrm(ks[16], (DEPTH, D_FF, D_MODEL), D_FF ** -0.5),
    }

def reference(x, norm_mix_g, w_in, q_norm_a, k_norm_a, sink_a, t5_bias, q_norm_b, k_norm_b, rel_bias_b, w_branch_a, w_branch_b, w_out, norm_ffn_g, w_ffn_gate, w_ffn_up, w_ffn_down):
    sizes = (A_QW, A_KVW, A_KVW, B_W, B_W, B_W, D_MODEL, D_MODEL)
    offsets = np.cumsum(sizes)[:-1].tolist()
    h = x
    for l in range(DEPTH):
        xn = rms_norm(h, norm_mix_g[l])
        proj = xn @ w_in[l]
        q_a, k_a, v_a, q_b, k_b, v_b, g_a, g_b = jnp.split(proj, offsets, axis=-1)
        o_a = mixer_a(q_a, k_a, v_a, q_norm_a[l], k_norm_a[l], sink_a[l], t5_bias)
        o_b = mixer_b(q_b, k_b, v_b, q_norm_b[l], k_norm_b[l], rel_bias_b[l])
        merged = jax.nn.sigmoid(g_a) * (o_a @ w_branch_a[l]) + jax.nn.sigmoid(g_b) * (o_b @ w_branch_b[l])
        h = h + merged @ w_out[l]
        hn = rms_norm(h, norm_ffn_g[l])
        h = h + (jax.nn.silu(hn @ w_ffn_gate[l]) * (hn @ w_ffn_up[l])) @ w_ffn_down[l]
    return h


_drawn_inputs = setup_inputs


def setup_inputs(seed=0):
    import zlib

    import numpy as np

    out = dict(_drawn_inputs(seed))
    spreads = {}
    factors = {'norm_mix_g': 8.0,
     'q_norm_a': 8.0,
     'k_norm_a': 8.0,
     'sink_a': 8.0,
     'q_norm_b': 8.0,
     'k_norm_b': 8.0,
     'norm_ffn_g': 3.788}
    for name, (base, spread) in spreads.items():
        noise = np.random.default_rng([zlib.crc32(name.encode()), seed]).standard_normal(out[name].shape)
        drawn = base * np.exp(spread * noise) if base else spread * noise
        out[name] = __import__('jax').numpy.asarray(drawn.astype(out[name].dtype))
    for name, factor in factors.items():
        out[name] = (out[name] * factor).astype(out[name].dtype)
    return out
```

```python
from contextlib import ExitStack

import numpy as np

import concourse.bass as bass
from concourse import mybir

F32 = mybir.dt.float32
F32R = mybir.dt.float32r
ACT = mybir.ActivationFunctionType
ALU = mybir.AluOpType
AX = mybir.AxisListType

P = 128
COLS = 512
HD = 64
GROUP = COLS // P
PIECE_KT = 2
CHUNK_KT = 4
RAW_SLOTS = 4
SPLIT_SLOTS = 4
EPS = 1e-6
NEG = -1e30
REL = 384
BIAS_SLOTS = 4


class Job:

    def __init__(self, kind, n, weight, row0, col0, cols, kts, lhs, kt0, pair):
        self.kind, self.n, self.weight, self.row0, self.col0, self.cols = kind, n, weight, row0, col0, cols
        self.kts, self.lhs, self.kt0, self.pair = kts, lhs, kt0, pair
        self.pieces = kts // PIECE_KT


def plan(d, qa, kva, qb, dff):
    kt = d // P
    kb = qa // P
    jobs = []
    pair = [0]

    def job(kind, n, weight, row0, col0, cols, kts, lhs, kt0, at=None):
        p = at
        if p is None:
            p = pair[0]
            pair[0] ^= 1
        jobs.append(Job(kind, n, weight, row0, col0, cols, kts, lhs, kt0, p))

    kv0 = qa
    b0 = qa + 2 * kva
    for n in range(qa // COLS):
        job("qk", n, "w_in", 0, n * COLS, COLS, kt, "x", 0)
    job("kv", 0, "w_in", 0, kv0, 2 * kva, kt, "x", 0)
    for n in range(2 * qb // COLS):
        job("qk", n + qa // COLS, "w_in", 0, b0 + n * COLS, COLS, kt, "x", 0)
    for n in range(qb // COLS):
        job("v", n, "w_in", 0, b0 + 2 * qb + n * COLS, COLS, kt, "x", 0)
    ga0 = b0 + 3 * qb
    for n in range(d // COLS):
        job("ga", n, "w_in", 0, ga0 + n * COLS, COLS, kt, "x", 0)
    for n in range(d // COLS):
        job("gb", n, "w_in", 0, ga0 + d + n * COLS, COLS, kt, "x", 0, 0)
        job("ba", n, "w_branch_a", 0, n * COLS, COLS, kb, "o", 0, 1)
        job("bb", n, "w_branch_b", 0, n * COLS, COLS, kb, "o", kb, 2)
    pair[0] = 0
    for n in range(d // COLS):
        job("out", n, "w_out", 0, n * COLS, COLS, kt, "m", 0)
    ff, s = 0, 0
    while ff < dff // COLS:
        k = min(4, dff // COLS - ff)
        for n in range(k):
            job("gate", ff + n, "w_ffn_gate", 0, (ff + n) * COLS, COLS, kt, "h", 0)
            job("up", ff + n, "w_ffn_up", 0, (ff + n) * COLS, COLS, kt, "h", 0)
            jobs[-1].slot = n
        for n in range(d // COLS):
            job("down", n, "w_ffn_down", ff * COLS, n * COLS, COLS, k * GROUP, "f", 0)
            jobs[-1].last = ff + k == dff // COLS
            jobs[-1].s = s
        ff += k
        s += 1
    piece = 0
    used = [0, 0, 0]
    sets = 0
    for j in jobs:
        j.piece0 = piece
        piece += j.pieces
        j.use = used[j.pair]
        used[j.pair] += 1
        if j.kind in ("qk", "kv", "bb", "out", "up"):
            j.set = sets
            sets += 1
    return jobs


def build(nc, x, norm_mix_g, w_in, q_norm_a, k_norm_a, sink_a, t5_bias, q_norm_b, k_norm_b, rel_bias_b,
          w_branch_a, w_branch_b, w_out, norm_ffn_g, w_ffn_gate, w_ffn_up, w_ffn_down, onehot, out):
    _, S, D = x.shape
    T = S // P
    KT = D // P
    QA = w_branch_a.shape[1]
    QB = w_branch_b.shape[1]
    KVA = (w_in.shape[2] - QA - 3 * QB - 2 * D) // 2
    DFF = w_ffn_gate.shape[2]
    HA, HB = QA // HD, QB // HD
    KVH = KVA // HD
    NPAIR_A, NPAIR_B = QA // P, QB // P
    assert T == 2 and KVA == P and QA == QB and HA == t5_bias.shape[1]
    jobs = plan(D, QA, KVA, QB, DFF)
    weights = {"w_in": w_in, "w_branch_a": w_branch_a, "w_branch_b": w_branch_b, "w_out": w_out,
               "w_ffn_gate": w_ffn_gate, "w_ffn_up": w_ffn_up, "w_ffn_down": w_ffn_down}
    NATT = NPAIR_A + NPAIR_B
    E0 = next(i for i, j in enumerate(jobs) if j.kind == "ga")
    ATT_PIECE0 = jobs[E0].piece0
    NCH = (jobs[-1].piece0 + jobs[-1].pieces) // 2
    XSETS = KT // GROUP

    ctx = ExitStack()
    with ctx:
        top = [nc.sbuf_base + (-nc.sbuf_base) % 64]

        def at(name, shape, dt, offset):
            return nc.alloc_sbuf_tensor_at(name, shape, dt, offset=offset)

        def take(n):
            o = top[0]
            top[0] += n + (-n) % 32
            return o

        def sb(name, shape, dt=F32):
            n = int(np.prod(shape[1:])) * 4
            return at(name, shape, dt, take(n))

        def sem(name):
            return ctx.enter_context(nc.semaphore(name))

        raw = sb("raw", [P, RAW_SLOTS, CHUNK_KT * COLS])
        w_hi = sb("w_hi", [P, SPLIT_SLOTS, PIECE_KT * COLS], F32R)
        w_lo = sb("w_lo", [P, SPLIT_SLOTS, PIECE_KT * COLS], F32R)
        xT_hi = sb("xT_hi", [P, KT, S], F32R)
        xT_lo = sb("xT_lo", [P, KT, S], F32R)
        o_oT = top[0]
        oT_hi = sb("oT_hi", [P, KT, S], F32R)
        oT_lo = sb("oT_lo", [P, KT, S], F32R)
        sqx = at("sqx", [P, T, D], F32, o_oT)
        o_att = take(2 * KT * S * 4)
        qT = at("qT", [P, NPAIR_A + 2 * NPAIR_B, S], F32, o_att)
        kT_a = at("kT_a", [P, KVH, S], F32, o_att + (NPAIR_A + 2 * NPAIR_B) * S * 4)
        mT_hi = at("mT_hi", [P, KT, S], F32R, o_att)
        mT_lo = at("mT_lo", [P, KT, S], F32R, o_att + KT * S * 4)
        o_v = take(T * (QB + KVA) * 4)
        o_bias = take(BIAS_SLOTS * 2 * 2 * P * 4)
        v_b = at("v_b", [P, T, QB], F32, o_v)
        v_a = at("v_a", [P, T, KVA], F32, o_v + T * QB * 4)
        o_ga = take(T * D * 4)
        x0 = at("x0", [P, T, D], F32, o_ga)
        gate_a = at("gate_a", [P, T, D], F32, o_ga)
        o_p = take(2 * 2 * 3 * P * 4)
        o_pt = take(2 * 2 * 3 * P * 4)
        bias = at("bias", [P, BIAS_SLOTS, 2, 2 * P], F32, o_bias)
        prob = at("prob", [P, 2, 2, 3 * P], F32, o_p)
        probT = at("probT", [P, 2, 2, 3 * P], F32, o_pt)
        h = at("h", [P, T, D], F32, o_v)
        tm = at("tm", [P, T, COLS], F32, o_p)
        sq = at("sq", [P, T, COLS], F32, o_p + T * COLS * 4)
        staged = at("staged", [P, T, COLS], F32, o_p + 2 * T * COLS * 4)
        full = staged
        ident = sb("ident", [P, P])
        NG = 2 * KT + 4
        g_rows = sb("g_rows", [NG, P])
        g_col = sb("g_col", [P, NG])
        gq = sb("gq", [P, 2])
        sink = sb("sink", [P, HA])
        t5 = sb("t5", [t5_bias.shape[0], HA])
        oneh = at("oneh", [t5_bias.shape[0], REL], F32, o_v)
        tab = at("tab", [HA, REL], F32, o_v + REL * 4)
        neghalf = sb("neghalf", [P, 16])
        ssx = sb("ssx", [P, T])
        ssx2 = sb("ssx2", [P, T])
        rx = sb("rx", [P, T])
        ssh = sb("ssh", [P, T, D // COLS])
        ssh1 = sb("ssh1", [P, T])
        ssh2 = sb("ssh2", [P, T])
        rh = sb("rh", [P, T])
        ssq = sb("ssq", [P, 16])
        ssq2 = sb("ssq2", [P, 16])
        rq = sb("rq", [P, 16])
        mx = sb("mx", [P, 2, 4])
        nmx = sb("nmx", [P, 2, 4])
        rs = sb("rs", [P, 2, 4])
        sd = sb("sd", [P, 2, 4])
        es = sb("es", [P, 2, 4])
        den = sb("den", [P, 2, 4])
        rden = sb("rden", [P, 2, 4])
        assert top[0] <= nc.sbuf_usable_end
        table = nc.dram_tensor("bias_table_a", [HA, REL], F32, kind="Internal").ap()

        bank = [ctx.enter_context(nc.psum_tensor(f"bank{i}", [P, COLS], F32)) for i in range(8)]

        landed = [sem(f"landed{i}") for i in range(RAW_SLOTS)]
        hi_ready = sem("hi_ready")
        lo_ready = sem("lo_ready")
        piece_used = sem("piece_used")
        x_landed = [sem(f"x_landed{i}") for i in range(XSETS)]
        g_landed = sem("g_landed")
        sink_landed = sem("sink_landed")
        t5_landed = sem("t5_landed")
        tab_stored = sem("tab_stored")
        bias_landed = [sem(f"bias_landed{i}") for i in range(BIAS_SLOTS)]
        h_landed = sem("h_landed")
        out_stored = sem("out_stored")
        ident_ready = sem("ident_ready")
        masks_ready = sem("masks_ready")
        g_turned = sem("g_turned")
        g_ready = sem("g_ready")
        tab_made = sem("tab_made")
        tab_copied = sem("tab_copied")
        pool_chain = sem("pool_chain")
        ssx_ready = sem("ssx_ready")
        rx_ready = sem("rx_ready")
        ssh_ready = sem("ssh_ready")
        ssh_sum = sem("ssh_sum")
        rh_ready = sem("rh_ready")
        xset_done = sem("xset_done")
        full_ready = sem("full_ready")
        full_hi = sem("full_hi")
        xT_ready = sem("xT_ready")
        tm_ready = sem("tm_ready")
        ssq_ready = sem("ssq_ready")
        rq_ready = sem("rq_ready")
        staged_ready = sem("staged_ready")
        tp_done = sem("tp_done")
        qk_ready = sem("qk_ready")
        v_ready = sem("v_ready")
        s_done = sem("s_done")
        s_read = sem("s_read")
        nmx_ready = sem("nmx_ready")
        exp_done = sem("exp_done")
        p_ready = sem("p_ready")
        pt_done = sem("pt_done")
        pt_read_a = sem("pt_read_a")
        pt_read_d = sem("pt_read_d")
        o_done = sem("o_done")
        o_hi = sem("o_hi")
        o_ready = sem("o_ready")
        tp_hi = sem("tp_hi")
        ga_ready = sem("ga_ready")
        ga_sig = sem("ga_sig")
        gb_sig = sem("gb_sig")
        m1_done = sem("m1_done")
        m_ready = sem("m_ready")
        h_ready = sem("h_ready")
        h_added = sem("h_added")
        staged_f = sem("staged_f")
        mT_ready = sem("mT_ready")
        fT_ready = sem("fT_ready")
        f_sig = sem("f_sig")
        f_ready = sem("f_ready")
        dve_chain = sem("dve_chain")

        block = ctx.enter_context(nc.Block())
        lhs = {"x": (xT_hi, xT_lo), "o": (oT_hi, oT_lo), "m": (mT_hi, mT_lo), "h": (xT_hi, xT_lo),
               "f": (oT_hi, oT_lo)}
        count = {"bb": 0, "out": 0, "up": 0}
        for j in jobs:
            if j.kind in count:
                j.group = count[j.kind]
                count[j.kind] += 1
        SET_OUT0 = next(j.set for j in jobs if j.kind == "bb")

        def evacuated(j):
            return {"qk": lambda: (tm_ready, j.set + 1), "kv": lambda: (tm_ready, j.set + 1),
                    "v": lambda: (v_ready, j.n + 1), "ga": lambda: (ga_ready, j.n + 1),
                    "gb": lambda: (gb_sig, T * (j.n + 1)), "ba": lambda: (m1_done, T * (j.n + 1)),
                    "bb": lambda: (m_ready, j.n + 1), "out": lambda: (h_ready, j.n + 1),
                    "gate": lambda: (f_ready, T * (j.n + 1)), "up": lambda: (staged_f, j.n + 1),
                    "down": lambda: (h_added, j.s * (D // COLS) + j.n + 1)}[j.kind]()

        def set_read(j):
            return {"qk": lambda: (qk_ready, T * (j.set + 1)), "kv": lambda: (qk_ready, T * (j.set + 1)),
                    "bb": lambda: (mT_ready, T * (j.n + 1)), "out": lambda: (full_ready, XSETS + j.n + 1),
                    "up": lambda: (fT_ready, T * (j.n + 1))}[j.kind]()

        def att_pair(i):
            b, n = i % 2, i // 2
            return b, n

        @block.sync
        def _(sp):
            def chunk(c, w, row0, col0, cols):
                slot = c % RAW_SLOTS
                if c >= RAW_SLOTS:
                    sp.wait_ge(lo_ready, 2 * (c - RAW_SLOTS) + 2)
                src = w[0, row0:row0 + CHUNK_KT * P, col0:col0 + cols].rearrange("(k p) n -> p k n", p=P)
                dst = raw[:, slot, 0:CHUNK_KT * cols].rearrange("p (k n) -> p k n", n=cols)
                sp.dma_start(dst, src).then_inc(landed[slot], 16)

            def load_bias(i):
                b, n = att_pair(i)
                slot = i % BIAS_SLOTS
                if i >= BIAS_SLOTS:
                    sp.wait_ge(s_read, i - BIAS_SLOTS + 1)
                hp = P // 2
                if b:
                    t, pitch, off, c0, lo, hi = rel_bias_b, rel_bias_b.shape[2], 1, 0, 2 * P, 3 * HD
                    base = 2 * n * pitch + off
                    parts = ((0, 0, 4 * HD), (hp, 0, 3 * HD))
                else:
                    t, pitch = table, REL
                    base = 2 * n * pitch
                    parts = ((0, 2 * HD, 2 * HD), (hp, HD, 2 * HD))
                for p0, c, w in parts:
                    src = bass.AP(t.tensor, t.offset + base + p0 + c, [[1, hp], [pitch, 2], [1, w]])
                    sp.dma_start(bias[p0:p0 + hp, slot, :, c:c + w], src).then_inc(bias_landed[slot], 16)

            xv = x[0].rearrange("(t p) d -> p t d", p=P)
            for g in range(XSETS):
                cs = slice(g * COLS, (g + 1) * COLS)
                sp.dma_start(x0[:, :, cs], xv[:, :, cs]).then_inc(x_landed[g], 16)
                if g == 0:
                    sp.dma_start(g_rows[0:KT, :], norm_mix_g[0].rearrange("(k p) -> k p", p=P)).then_inc(g_landed, 16)
                    sp.dma_start(g_rows[KT:2 * KT, :], norm_ffn_g[0].rearrange("(k p) -> k p", p=P)).then_inc(g_landed, 16)
                    for r, g1 in enumerate((q_norm_a, k_norm_a, q_norm_b, k_norm_b)):
                        for s in range(2):
                            sp.dma_start(g_rows[2 * KT + r:2 * KT + r + 1, s * HD:(s + 1) * HD], g1).then_inc(g_landed, 16)
            c = 0
            for ji, j in enumerate(jobs):
                for q in range(j.pieces // 2):
                    chunk(c, weights[j.weight], j.row0 + q * CHUNK_KT * P, j.col0, j.cols)
                    if c == 3:
                        sp.dma_start(sink[:], bass.AP(sink_a.tensor, sink_a.offset, [[0, P], [1, HA]])).then_inc(sink_landed, 16)
                        sp.dma_start(t5[:], t5_bias).then_inc(t5_landed, 16)
                        sp.dma_start(oneh[:], onehot).then_inc(t5_landed, 16)
                    if c == 8:
                        sp.wait_ge(tab_copied, 1)
                        sp.dma_start(table, tab[:]).then_inc(tab_stored, 16)
                        sp.wait_ge(tab_stored, 16)
                        sp.wait_ge(masks_ready, 1)
                    i = c - 3 - ATT_PIECE0 // 2
                    if 0 <= i < NATT:
                        load_bias(i)
                    c += 1
                if j.kind == "bb" and j.n == 0:
                    sp.wait_ge(o_ready, NATT)
                    sp.dma_start(h[:], xv).then_inc(h_landed, 16)
            ov = out[0].rearrange("(t p) d -> p t d", p=P)
            for n in range(D // COLS):
                sp.wait_ge(h_added, (jobs[-1].s) * (D // COLS) + n + 1)
                cs = slice(n * COLS, (n + 1) * COLS)
                sp.dma_start(ov[:, :, cs], h[:, :, cs]).then_inc(out_stored, 16)
            sp.wait_ge(out_stored, 16 * (D // COLS))

        @block.gpsimd
        def _(pool):
            chain = [0]

            def link(ins):
                chain[0] += 1
                ins.then_inc(pool_chain, 1)
                pool.wait_ge(pool_chain, chain[0])

            link(nc.gpsimd.memset(ident[:], 0.0))
            nc.gpsimd.affine_select(out=ident[:], in_=ident[:], compare_op=ALU.not_equal, fill=1.0, base=0,
                                    pattern=[[-1, P]], channel_multiplier=1).then_inc(ident_ready, 1)
            link(nc.gpsimd.memset(neghalf[:], -0.5))

            def rsqrt(dst, mid, src, n, width, ready):
                link(nc.gpsimd.tensor_scalar(mid, src, 1.0 / n, EPS, ALU.mult, ALU.add))
                nc.gpsimd.tensor_tensor(dst, mid, neghalf[:, 0:width], ALU.pow).then_inc(ready, 1)

            pool.wait_ge(ssx_ready, T)
            rsqrt(rx[:], ssx2[:], ssx[:], D, T, rx_ready)
            for n, j in enumerate(j for j in jobs if j.kind in ("qk", "kv")):
                pool.wait_ge(ssq_ready, n + 1)
                wd = T * (COLS // HD) if j.kind == "qk" else T * KVH
                if n:
                    pool.wait_ge(staged_ready, n)
                rsqrt(rq[:, 0:wd], ssq2[:, 0:wd], ssq[:, 0:wd], HD, wd, rq_ready)
            pool.wait_ge(ssh_sum, 1)
            rsqrt(rh[:], ssh2[:], ssh1[:], D, T, rh_ready)

        @block.scalar
        def _(act):
            A = nc.scalar.activation

            def hi(j, k):
                p = j.piece0 + k
                c = p // 2
                act.wait_ge(landed[c % RAW_SLOTS], 16 * (c // RAW_SLOTS + 1))
                if p >= SPLIT_SLOTS:
                    act.wait_ge(piece_used, p - SPLIT_SLOTS + 1)
                w = PIECE_KT * j.cols
                A(w_hi[:, p % SPLIT_SLOTS, 0:w], raw[:, c % RAW_SLOTS, (p % 2) * w:(p % 2) * w + w],
                  ACT.Copy).then_inc(hi_ready, 1)

            def job_done(j):
                act.wait_ge(piece_used, j.piece0 + j.pieces)

            def evac_scaled(j, dst, rows, scale):
                for t in range(T):
                    ins = A(dst(t), bank[2 * j.pair + t][:, rows], ACT.Copy, scale=scale[:, t:t + 1])
                return ins

            def x_hi(g):
                act.wait_ge(full_ready, g + 1)
                A(xT_hi[:, g * GROUP:(g + 1) * GROUP, :].rearrange("p k (t s) -> p t k s", t=T),
                  full[:].rearrange("p t (k s) -> p t k s", k=GROUP), ACT.Copy).then_inc(full_hi, 1)

            def rows_hi(j, dst, g):
                act.wait_ge(tp_done, j.set + 1)
                for t in range(T):
                    A(dst[:, g * GROUP:(g + 1) * GROUP, t * P:(t + 1) * P],
                      bank[6 + t][:].rearrange("p (k s) -> p k s", k=GROUP), ACT.Copy).then_inc(tp_hi, 1)

            def side(j, k, nxt):
                if j is None:
                    if k < XSETS:
                        x_hi(k)
                    return
                last = nxt.pieces - 1
                if j.kind in ("qk", "kv"):
                    if k == 3:
                        job_done(j)
                        if j.set == 0:
                            act.wait_ge(rx_ready, 1)
                        else:
                            act.wait_ge(staged_ready, j.set)
                        if j.kind == "qk":
                            evac_scaled(j, lambda t: tm[:, t, :], slice(0, COLS), rx).then_inc(tm_ready, 1)
                        else:
                            evac_scaled(j, lambda t: v_a[:, t, :], slice(KVA, 2 * KVA), rx)
                            evac_scaled(j, lambda t: tm[:, t, 0:KVA], slice(0, KVA), rx).then_inc(tm_ready, 1)
                    if k == 7:
                        act.wait_ge(tp_done, j.set + 1)
                        for t in range(T):
                            if j.kind == "qk":
                                b = j.n >= QA // COLS
                                isq = j.n < (QA + QB) // COLS
                                sc = gq[:, b:b + 1] if isq else g_col[:, 2 * KT + 3:2 * KT + 4]
                                dst = qT[:, j.n * GROUP:(j.n + 1) * GROUP, t * P:(t + 1) * P]
                                ins = A(dst[:, :, ::-1] if isq else dst,
                                        bank[6 + t][:].rearrange("p (k s) -> p k s", k=GROUP), ACT.Copy, scale=sc)
                            else:
                                ins = A(kT_a[:, :, t * P:(t + 1) * P],
                                        bank[6 + t][:, 0:KVH * P].rearrange("p (k s) -> p k s", k=KVH), ACT.Copy,
                                        scale=g_col[:, 2 * KT + 1:2 * KT + 2])
                            ins.then_inc(qk_ready, 1)
                if j.kind == "v" and k == 3:
                    job_done(j)
                    act.wait_ge(tab_stored, 16)
                    evac_scaled(j, lambda t: v_b[:, t, j.n * COLS:(j.n + 1) * COLS], slice(0, COLS), rx)\
                        .then_inc(v_ready, 1)
                if j.kind == "ga" and k == 3:
                    job_done(j)
                    if j.n == 0:
                        act.wait_ge(xset_done, XSETS)
                    evac_scaled(j, lambda t: gate_a[:, t, j.n * COLS:(j.n + 1) * COLS], slice(0, COLS), rx)\
                        .then_inc(ga_ready, 1)
                if j.kind == "gb" and k == 3:
                    job_done(j)
                    if j.n:
                        act.wait_ge(m_ready, j.n)
                    for t in range(T):
                        ga = gate_a[:, t, j.n * COLS:(j.n + 1) * COLS]
                        act.wait_ge(ga_ready, j.n + 1)
                        A(ga, ga, ACT.Sigmoid).then_inc(ga_sig, 1)
                        A(tm[:, t, :], bank[2 * j.pair + t][:], ACT.Sigmoid, scale=rx[:, t:t + 1]).then_inc(gb_sig, 1)
                if j.kind == "bb" and k == 5:
                    rows_hi(j, mT_hi, j.n)
                if j.kind == "out":
                    if k == 4:
                        act.wait_ge(h_ready, j.n + 1)
                        for t in range(T):
                            A(sq[:, t, :], h[:, t, j.n * COLS:(j.n + 1) * COLS], ACT.Square,
                              accum_out=ssh[:, t, j.n:j.n + 1]).then_inc(ssh_ready, 1)
                        act.wait_ge(ssh_ready, T * (j.n + 1))
                    if k == 6:
                        act.wait_ge(full_ready, XSETS + j.n + 1)
                        A(xT_hi[:, j.n * GROUP:(j.n + 1) * GROUP, :].rearrange("p k (t s) -> p t k s", t=T),
                          full[:].rearrange("p t (k s) -> p t k s", k=GROUP), ACT.Copy).then_inc(full_hi, 1)
                if j.kind == "gate" and k == 3:
                    job_done(j)
                    if j.n == 0:
                        act.wait_ge(rh_ready, 1)
                    else:
                        act.wait_ge(f_ready, 2 * j.n)
                    for t in range(T):
                        A(tm[:, t, :], bank[2 * j.pair + t][:], ACT.Sigmoid, scale=rh[:, t:t + 1]).then_inc(f_sig, 1)
                if j.kind == "up" and k == 5:
                    rows_hi(j, oT_hi, j.slot)

            def exp_probs(i):
                b, n = att_pair(i)
                s = i % 2
                act.wait_ge(nmx_ready, i + 1)
                for e in range(2):
                    for t in range(2):
                        v = prob[:, s, e, 0:2 * P] if t else prob[:, s, e, 2 * P:3 * P]
                        q = 2 * e + t
                        A(v, v, ACT.Exp, bias=nmx[:, s, q:q + 1], accum_out=rs[:, s, q:q + 1]).then_inc(exp_done, 1)
                A(es[:, s, :], sd[:, s, :], ACT.Exp).then_inc(exp_done, 1)

            def pt_copy(i):
                act.wait_ge(pt_done, i + 1)
                A(probT[:, i % 2, 0, :], bank[6][:, 0:3 * P], ACT.Copy).then_inc(pt_read_a, 1)

            def o_copy(i):
                b, n = att_pair(i)
                act.wait_ge(o_done, i + 1)
                A(oT_hi[:, b * NPAIR_A + n, :], bank[6][:, 0:S], ACT.Copy).then_inc(o_hi, 1)

            prev = None
            for ji, j in enumerate(jobs):
                for k in range(j.pieces):
                    hi(j, k)
                    if ji == 0 and k == 4:
                        for g in range(XSETS):
                            act.wait_ge(x_landed[g], 16)
                        for t in range(T):
                            A(sqx[:, t, :], x0[:, t, :], ACT.Square, accum_out=ssx[:, t:t + 1]).then_inc(ssx_ready, 1)
                    side(prev, k, j)
                    a = j.piece0 + k - ATT_PIECE0 - SPLIT_SLOTS
                    if 0 <= a and a // 2 < NATT and a % 2 == 0:
                        exp_probs(a // 2)
                    a2 = a - 1 - 2
                    if a % 2 == 0 and 1 <= a // 2 <= NATT:
                        pt_copy(a // 2 - 1)
                    if a % 2 == 1 and 1 <= a // 2 <= NATT:
                        o_copy(a // 2 - 1)
                prev = j

        @block.vector
        def _(dve):
            V = nc.vector
            chain = [0]

            def link(ins):
                chain[0] += 1
                ins.then_inc(dve_chain, 1)
                dve.wait_ge(dve_chain, chain[0])

            def lo(j, k):
                p = j.piece0 + k
                c = p // 2
                dve.wait_ge(hi_ready, p + 1)
                w = PIECE_KT * j.cols
                V.tensor_tensor(w_lo[:, p % SPLIT_SLOTS, 0:w], raw[:, c % RAW_SLOTS, (p % 2) * w:(p % 2) * w + w],
                                w_hi[:, p % SPLIT_SLOTS, 0:w].bitcast(F32), ALU.subtract).then_inc(lo_ready, 1)

            def full_rows(banks, gcol0, n):
                if n:
                    dve.wait_ge(xT_ready, n)
                for t in range(T):
                    ins = V.tensor_tensor(full[:, t, :].rearrange("p (k s) -> p k s", k=GROUP),
                                          banks[t][:].rearrange("p (k s) -> p k s", k=GROUP),
                                          g_col[:, gcol0:gcol0 + GROUP, None].to_broadcast([P, GROUP, P]), ALU.mult)
                    if t == 0:
                        ins.then_inc(dve_chain, 1)
                        chain[0] += 1
                ins.then_inc(full_ready, 1)

            def full_lo(n, g):
                dve.wait_ge(full_hi, n + 1)
                V.tensor_tensor(xT_lo[:, g * GROUP:(g + 1) * GROUP, :].rearrange("p k (t s) -> p t k s", t=T),
                                full[:].rearrange("p t (k s) -> p t k s", k=GROUP),
                                xT_hi[:, g * GROUP:(g + 1) * GROUP, :].bitcast(F32).rearrange("p k (t s) -> p t k s", t=T),
                                ALU.subtract).then_inc(xT_ready, 1)

            def rows_lo(j, dst_hi, dst_lo, g, hi0, ready):
                for t in range(T):
                    dve.wait_ge(tp_hi, hi0 + t + 1)
                    ins = V.tensor_tensor(dst_lo[:, g * GROUP:(g + 1) * GROUP, t * P:(t + 1) * P],
                                          bank[6 + t][:].rearrange("p (k s) -> p k s", k=GROUP),
                                          dst_hi[:, g * GROUP:(g + 1) * GROUP, t * P:(t + 1) * P].bitcast(F32),
                                          ALU.subtract)
                    ins.then_inc(ready, 1)

            def side(j, k):
                if j is None:
                    return
                if j.kind in ("qk", "kv"):
                    nh = COLS // HD if j.kind == "qk" else KVH
                    w = nh * HD
                    if k == 3:
                        dve.wait_ge(tm_ready, j.set + 1)
                        link(V.tensor_tensor(sq[:, :, 0:w], tm[:, :, 0:w], tm[:, :, 0:w], ALU.mult))
                        if j.set:
                            dve.wait_ge(rq_ready, j.set)
                        V.tensor_reduce(ssq[:, 0:T * nh], sq[:, :, 0:w].rearrange("p t (h d) -> p t h d", d=HD),
                                        AX.X, ALU.add).then_inc(ssq_ready, 1)
                    if k == 5:
                        dve.wait_ge(rq_ready, j.set + 1)
                        if j.set:
                            dve.wait_ge(tp_done, j.set)
                        src = tm[:, :, 0:w].rearrange("p t (h d) -> p t h d", d=HD)
                        r = rq[:, 0:T * nh].rearrange("p (t h) -> p t h", t=T)[:, :, :, None].to_broadcast([P, T, nh, HD])
                        if j.kind == "qk":
                            V.tensor_tensor(staged[:].rearrange("p t (h d) -> p t h d", d=HD), src, r,
                                            ALU.mult).then_inc(staged_ready, 1)
                        else:
                            dst = staged[:, :, 0:2 * w].rearrange("p t (h c d) -> p t h c d", h=nh, c=2)
                            link(V.tensor_tensor(dst[:, :, :, 0, :], src, r, ALU.mult))
                            V.tensor_tensor(dst[:, :, :, 1, :], src, r, ALU.mult).then_inc(staged_ready, 1)
                cs = slice(j.n * COLS, (j.n + 1) * COLS)
                if j.kind == "ba" and k == 3:
                    dve.wait_ge(piece_used, j.piece0 + j.pieces)
                    if j.n:
                        dve.wait_ge(m_ready, j.n)
                    dve.wait_ge(ga_sig, T * (j.n + 1))
                    for t in range(T):
                        V.tensor_tensor(sq[:, t, :], bank[2 * j.pair + t][:], gate_a[:, t, cs], ALU.mult)\
                            .then_inc(m1_done, 1)
                if j.kind == "bb" and k == 3:
                    dve.wait_ge(piece_used, j.piece0 + j.pieces)
                    dve.wait_ge(gb_sig, T * (j.n + 1))
                    dve.wait_ge(tp_done, j.set)
                    for t in range(T):
                        ins = V.tensor_tensor(tm[:, t, :], bank[2 * j.pair + t][:], tm[:, t, :], ALU.mult)
                        link(ins)
                    V.tensor_tensor(staged[:], tm[:], sq[:], ALU.add).then_inc(m_ready, 1)
                if j.kind == "bb" and k == 5:
                    rows_lo(j, mT_hi, mT_lo, j.n, T * j.n, mT_ready)
                if j.kind == "out":
                    if k == 3:
                        dve.wait_ge(piece_used, j.piece0 + j.pieces)
                        dve.wait_ge(h_landed, 16)
                        for t in range(T):
                            ins = V.tensor_tensor(h[:, t, cs], bank[2 * j.pair + t][:], h[:, t, cs], ALU.add)
                            if t == 0:
                                link(ins)
                        ins.then_inc(h_ready, 1)
                    if k == 5:
                        dve.wait_ge(tp_done, j.set + 1)
                        full_rows(bank[6:8], KT + j.n * GROUP, XSETS + j.n)
                        if j.n == D // COLS - 1:
                            dve.wait_ge(ssh_ready, T * (j.n + 1))
                            V.tensor_reduce(ssh1[:], ssh[:], AX.X, ALU.add).then_inc(ssh_sum, 1)
                    if k == 6:
                        full_lo(XSETS + j.n, j.n)
                if j.kind == "gate" and k == 3:
                    for t in range(T):
                        dve.wait_ge(f_sig, T * j.n + t + 1)
                        if t == 0 and j.n:
                            pass
                        V.scalar_tensor_tensor(sq[:, t, :], bank[2 * j.pair + t][:], rh[:, t:t + 1], tm[:, t, :],
                                               ALU.mult, ALU.mult).then_inc(f_ready, 1)
                if j.kind == "up":
                    if k == 3:
                        dve.wait_ge(piece_used, j.piece0 + j.pieces)
                        dve.wait_ge(tp_done, j.set)
                        for t in range(T):
                            ins = V.scalar_tensor_tensor(staged[:, t, :], bank[2 * j.pair + t][:], rh[:, t:t + 1],
                                                         sq[:, t, :], ALU.mult, ALU.mult)
                            if t == 0:
                                link(ins)
                        ins.then_inc(staged_f, 1)
                    if k == 5:
                        rows_lo(j, oT_hi, oT_lo, j.slot, T * (D // COLS) + T * j.n, fT_ready)
                if j.kind == "down" and k == 3:
                    down_add(j)

            def down_add(j):
                cs = slice(j.n * COLS, (j.n + 1) * COLS)
                dve.wait_ge(piece_used, j.piece0 + j.pieces)
                for t in range(T):
                    ins = V.tensor_tensor(h[:, t, cs], bank[2 * j.pair + t][:], h[:, t, cs], ALU.add)
                    if t == 0:
                        link(ins)
                ins.then_inc(h_added, 1)

            def softmax_in(i):
                b, n = att_pair(i)
                s = i % 2
                dve.wait_ge(s_done, i + 1)
                dve.wait_ge(bias_landed[i % BIAS_SLOTS], 32 * (i // BIAS_SLOTS + 1))
                if i == 0:
                    dve.wait_ge(sink_landed, 16)
                if i >= 2:
                    dve.wait_ge(pt_done, i - 1)
                for e in range(2):
                    for t in range(2):
                        q = 2 * e + t
                        dst = prob[:, s, e, 0:2 * P] if t else prob[:, s, e, 2 * P:3 * P]
                        src = bank[4 + e][:, 0:2 * P] if t else bank[4 + e][:, 2 * P:3 * P]
                        bs = bias[:, i % BIAS_SLOTS, e, :] if t else bias[:, i % BIAS_SLOTS, e, P:2 * P]
                        start = NEG if b else sink[:, 2 * n + e:2 * n + e + 1]
                        ins = V.tensor_tensor_reduce(out=dst, in0=src, in1=bs, scale=1.0, scalar=start, op0=ALU.add,
                                                     op1=ALU.max, accum_out=mx[:, s, q:q + 1])
                        if q < 3:
                            ins.then_inc(dve_chain, 1)
                            chain[0] += 1
                ins.then_inc(s_read, 1)
                dve.wait_ge(s_read, i + 1)
                if b:
                    link(V.memset(sd[:, s, :], NEG))
                else:
                    link(V.tensor_tensor(sd[:, s, :].rearrange("p (e t) -> p e t", t=2),
                                         sink[:, 2 * n:2 * n + 2, None].to_broadcast([P, 2, 2]),
                                         mx[:, s, :].rearrange("p (e t) -> p e t", t=2), ALU.subtract))
                V.tensor_scalar(nmx[:, s, :], mx[:, s, :], -1.0, None, ALU.mult).then_inc(nmx_ready, 1)

            def softmax_out(i):
                s = i % 2
                dve.wait_ge(exp_done, 5 * (i + 1))
                link(V.tensor_tensor(den[:, s, :], rs[:, s, :], es[:, s, :], ALU.add))
                link(V.reciprocal(rden[:, s, :], den[:, s, :]))
                for e in range(2):
                    for t in range(2):
                        v = prob[:, s, e, 0:2 * P] if t else prob[:, s, e, 2 * P:3 * P]
                        q = 2 * e + t
                        V.tensor_scalar(v, v, rden[:, s, q:q + 1], None, ALU.mult).then_inc(p_ready, 1)

            def pt_copy(i):
                dve.wait_ge(pt_done, i + 1)
                V.tensor_copy(probT[:, i % 2, 1, :], bank[7][:, 0:3 * P]).then_inc(pt_read_d, 1)

            def o_copy(i):
                b, n = att_pair(i)
                dve.wait_ge(o_hi, i + 1)
                V.tensor_tensor(oT_lo[:, b * NPAIR_A + n, :], bank[6][:, 0:S],
                                oT_hi[:, b * NPAIR_A + n, :].bitcast(F32), ALU.subtract).then_inc(o_ready, 1)

            hp = P // 2
            for slot in range(BIAS_SLOTS):
                if slot % 2:
                    ins = V.memset(bias[hp:P, slot, :, 3 * HD:], NEG)
                else:
                    V.memset(bias[0:hp, slot, :, 0:2 * HD], NEG)
                    V.memset(bias[hp:P, slot, :, 0:HD], NEG)
                    ins = V.memset(bias[hp:P, slot, :, 3 * HD:], NEG)
            ins.then_inc(masks_ready, 1)
            dve.wait_ge(g_turned, 1)
            V.tensor_copy(g_col[:], bank[0][:, 0:NG]).then_inc(g_ready, 1)
            dve.wait_ge(g_ready, 1)
            for b in range(2):
                V.tensor_scalar(gq[:, b:b + 1], g_col[:, 2 * KT + 2 * b:2 * KT + 2 * b + 1], float(HD) ** -0.5, None,
                                ALU.mult).then_inc(g_ready, 1)
            prev = None
            for ji, j in enumerate(jobs):
                for k in range(j.pieces):
                    if ji == 0 and k < XSETS:
                        dve.wait_ge(xset_done, k + 1)
                        full_rows(bank[4 + 2 * (k % 2):6 + 2 * (k % 2)], k * GROUP, k)
                    lo(j, k)
                    if ji == 0 and k < XSETS:
                        full_lo(k, k)
                    if ji == 0 and k == 6:
                        dve.wait_ge(tab_made, 1)
                        V.tensor_copy(tab[:], bank[2][0:HA, 0:REL]).then_inc(tab_copied, 1)
                    side(prev, k)
                    a = j.piece0 + k - ATT_PIECE0 - SPLIT_SLOTS + 1
                    if a >= 0 and a % 2 == 0 and a // 2 < NATT:
                        softmax_in(a // 2)
                    if a % 2 == 1 and 1 <= a // 2 <= NATT:
                        pt_copy(a // 2 - 1)
                    if a % 2 == 1 and 0 <= a // 2 < NATT:
                        softmax_out_at = a // 2
                    if a % 2 == 0 and 1 <= a // 2 - 1 <= NATT:
                        o_copy(a // 2 - 2)
                    if a % 2 == 1 and 0 <= a // 2 < NATT:
                        softmax_out(a // 2)
                prev = j
            down_add(prev)

        @block.tensor
        def _(pe):
            M = nc.tensor.matmul

            def scores(i):
                b, n = att_pair(i)
                if i == 0:
                    pe.wait_ge(qk_ready, T * 7)
                else:
                    pe.wait_ge(s_read, i)
                for t in (1, 0):
                    for e in range(2):
                        rows = slice(e * HD, (e + 1) * HD)
                        q = qT[rows, b * NPAIR_A + n, t * P:(t + 1) * P]
                        keys = slice(0, (t + 1) * P)
                        k = qT[rows, NPAIR_A + NPAIR_B + n, keys] if b else \
                            kT_a[rows, (2 * n) // (HA // KVH), keys]
                        o = bank[4 + e][:, 0:2 * P] if t else bank[4 + e][:, 2 * P:3 * P]
                        ins = M(o, q, k, start=True, stop=True)
                ins.then_inc(s_done, 1)

            def turn_probs(i):
                s = i % 2
                pe.wait_ge(p_ready, 4 * (i + 1))
                if i:
                    pe.wait_ge(o_ready, i)
                for e in range(2):
                    for c in range(3):
                        cs = slice(c * P, (c + 1) * P)
                        ins = nc.tensor.transpose(bank[6 + e][:, cs], prob[:, s, e, cs], ident[:])
                ins.then_inc(pt_done, 1)

            def values(i):
                b, n = att_pair(i)
                s = i % 2
                pe.wait_ge(pt_read_a, i + 1)
                pe.wait_ge(pt_read_d, i + 1)
                if i == 0:
                    pe.wait_ge(v_ready, QB // COLS)
                for e in range(2):
                    hcol = (2 * n + e) * HD if b else (2 * n // (HA // KVH)) * HD
                    v = v_b if b else v_a
                    vs = lambda kt: v[:, kt, hcol:hcol + HD]
                    rows = slice(e * HD, (e + 1) * HD)
                    pr = lambda c: probT[:, s, e, c * P:(c + 1) * P][:, ::-1]
                    M(bank[6][rows, 0:P], vs(0), pr(2), start=True, stop=True)
                    M(bank[6][rows, P:2 * P], vs(0), pr(0), start=True, stop=False)
                    ins = M(bank[6][rows, P:2 * P], vs(1), pr(1), start=False, stop=True)
                ins.then_inc(o_done, 1)

            def turn_set(j):
                before = next((b for b in jobs if hasattr(b, "set") and b.set == j.set - 1), None)
                if before:
                    pe.wait_ge(*set_read(before))
                nb = GROUP if j.kind != "kv" else KVH
                if j.kind in ("qk", "kv"):
                    pe.wait_ge(staged_ready, j.set + 1)
                elif j.kind == "bb":
                    pe.wait_ge(m_ready, j.n + 1)
                elif j.kind == "out":
                    pe.wait_ge(h_ready, j.n + 1)
                else:
                    pe.wait_ge(staged_f, j.n + 1)
                src = h[:, :, j.n * COLS:(j.n + 1) * COLS] if j.kind == "out" else staged
                for t in range(T):
                    for g in range(nb):
                        ins = nc.tensor.transpose(bank[6 + t][:, g * P:(g + 1) * P], src[:, t, g * P:(g + 1) * P],
                                                  ident[:])
                ins.then_inc(tp_done, 1)

            pe.wait_ge(ident_ready, 1)
            pe.wait_ge(g_landed, 16 * 10)
            nc.tensor.transpose(bank[0][:, 0:NG], g_rows[:], ident[0:NG, 0:NG]).then_inc(g_turned, 1)

            def x_set(g):
                pe.wait_ge(x_landed[g], 16)
                if g >= 2:
                    pe.wait_ge(full_ready, g - 1)
                for t in range(T):
                    for c in range(GROUP):
                        c0 = g * COLS + c * P
                        ins = nc.tensor.transpose(bank[4 + 2 * (g % 2) + t][:, c * P:(c + 1) * P], x0[:, t, c0:c0 + P],
                                                  ident[:])
                ins.then_inc(xset_done, 1)

            x_set(0)
            x_set(1)
            pe.wait_ge(g_ready, 1)
            prev = None
            for ji, j in enumerate(jobs):
                before = [b for b in jobs[:ji] if b.pair == j.pair]
                if before:
                    pe.wait_ge(*evacuated(before[-1]))
                if ji == 1:
                    pe.wait_ge(tab_copied, 1)
                L_hi, L_lo = lhs[j.lhs]
                for k in range(j.pieces):
                    p = j.piece0 + k
                    a = p - ATT_PIECE0
                    if a >= 0 and a % 2 == 0 and a // 2 < NATT:
                        scores(a // 2)
                    pe.wait_ge(lo_ready, p + 1)
                    for q in range(PIECE_KT):
                        kk = k * PIECE_KT + q
                        kt = j.kt0 + kk
                        if kk % GROUP == 0:
                            if ji == 0:
                                pe.wait_ge(xT_ready, kk // GROUP + 1)
                            if j.kind == "ba" and j.n == 0 and kk == 0:
                                pe.wait_ge(o_ready, NATT)
                            if j.kind == "out" and j.n == 0:
                                pe.wait_ge(mT_ready, T * (kk // GROUP + 1))
                            if j.kind == "gate" and j.n == 0:
                                pe.wait_ge(xT_ready, XSETS + kk // GROUP + 1)
                            if j.kind == "down" and j.n == 0:
                                pe.wait_ge(fT_ready, T * (4 * j.s + kk // GROUP + 1))
                        hi_w = w_hi[:, p % SPLIT_SLOTS, q * j.cols:(q + 1) * j.cols]
                        lo_w = w_lo[:, p % SPLIT_SLOTS, q * j.cols:(q + 1) * j.cols]
                        for t in range(T):
                            ts = slice(t * P, (t + 1) * P)
                            o = bank[2 * j.pair + t][:, 0:j.cols]
                            M(o, L_hi[:, kt, ts], hi_w, start=kk == 0, stop=False)
                            M(o, L_lo[:, kt, ts], hi_w, start=False, stop=False)
                            ins = M(o, L_hi[:, kt, ts], lo_w, start=False, stop=kk == j.kts - 1)
                    ins.then_inc(piece_used, 1)
                    if ji == 0 and k < XSETS - 2:
                        x_set(k + 2)
                    if ji == 0 and k == 5:
                        pe.wait_ge(t5_landed, 32)
                        M(bank[2][0:HA, 0:REL], t5[:], oneh[:], start=True, stop=True).then_inc(tab_made, 1)
                    if prev is not None and hasattr(prev, "set"):
                        if k == (4 if prev.kind in ("qk", "kv") else 1) :
                            turn_set(prev)
                    if a >= 0 and a % 2 == 0 and 1 <= a // 2 <= NATT:
                        turn_probs(a // 2 - 1)
                    if a >= 0 and a % 2 == 1 and 1 <= a // 2 <= NATT:
                        values(a // 2 - 1)
                prev = j


_INS = ["x", "norm_mix_g", "w_in", "q_norm_a", "k_norm_a", "sink_a", "t5_bias", "q_norm_b", "k_norm_b", "rel_bias_b",
        "w_branch_a", "w_branch_b", "w_out", "norm_ffn_g", "w_ffn_gate", "w_ffn_up", "w_ffn_down"]


def t5_one_hot(buckets, max_dist):
    rel = np.arange(REL) - 255
    nb = buckets // 2
    exact = nb // 2
    n = np.abs(rel)
    large = exact + (np.log(np.maximum(n, 1) / exact) / np.log(max_dist / exact) * (nb - exact)).astype(np.int32)
    bucket = (rel > 0) * nb + np.where(n < exact, n, np.minimum(large, nb - 1))
    return (np.arange(buckets)[:, None] == bucket[None, :]).astype(np.float32)


def kernel(**inputs):
    import concourse.bacc as bacc
    from concourse.bass_utils import run_bass_kernel_spmd

    nc = bacc.Bacc("TRN2", target_bir_lowering=False, num_devices=1)
    arrays, args = {}, []
    for name in _INS + ["onehot"]:
        a = t5_one_hot(32, 128) if name == "onehot" else np.ascontiguousarray(inputs[name])
        arrays[f"in_{name}"] = a
        args.append(nc.dram_tensor(f"in_{name}", a.shape, mybir.dt.from_np(a.dtype), kind="ExternalInput").ap())
    out = nc.dram_tensor("out", inputs["x"].shape, F32, kind="ExternalOutput").ap()
    build(nc, *args, out)
    r = run_bass_kernel_spmd(nc, [arrays], core_ids=[0])
    return r.results[0]["out"]
```

```python
from contextlib import ExitStack

import numpy as np

import concourse.bass as bass
from concourse import mybir

F32 = mybir.dt.float32
F32R = mybir.dt.float32r
ACT = mybir.ActivationFunctionType
ALU = mybir.AluOpType
AX = mybir.AxisListType

P = 128
COLS = 512
GROUP = COLS // P
HD = 64
PIECE_KT = 2
CHUNK_KT = 4
RAW_SLOTS = 4
SPLIT_SLOTS = 4
BIAS_SLOTS = 4
FF_BLOCKS = 4
EPS = 1e-6
NEG = -1e30
REL = 384
ORIGIN = 255


class Job:

    def __init__(self, kind, n, weight, row0, col0, cols, kts, lhs, kt0, pair):
        self.kind = kind
        self.n = n
        self.first = n == 0
        self.weight, self.row0, self.col0, self.cols = weight, row0, col0, cols
        self.kts, self.pieces = kts, kts // PIECE_KT
        self.lhs, self.kt0 = lhs, kt0
        self.pair = pair
        self.piece0 = 0
        self.off = 0
        self.set = None
        self.slot = 0
        self.done = 0
        self.prev = self.before = None


def stepped(a, b, i, deep=True):
    j = Job(a.kind, a.n + (b.n - a.n) * i, a.weight, a.row0, a.col0 + (b.col0 - a.col0) * i, a.cols, a.kts, a.lhs,
            a.kt0, a.pair)
    j.first = a.first
    j.piece0 = a.piece0
    j.off = (b.piece0 - a.piece0) * i
    j.slot = a.slot + (b.slot - a.slot) * i
    j.done = a.done + (b.done - a.done) * i
    if a.set is not None:
        j.set = a.set + (b.set - a.set) * i
    if deep:
        j.prev = stepped(a.prev, b.prev, i, False)
        j.before = stepped(a.before, b.before, i, False)
    return j


def plan(d, qa, kva, qb, dff):
    kt = d // P
    kb = qa // P
    jobs, segments = [], []
    turn = [0]

    def job(kind, n, weight, row0, col0, cols, kts, lhs, kt0, pair=None):
        if pair is None:
            pair = turn[0]
            turn[0] ^= 1
        jobs.append(Job(kind, n, weight, row0, col0, cols, kts, lhs, kt0, pair))
        return jobs[-1]

    b0 = qa + 2 * kva
    ga0 = b0 + 3 * qb
    job("kv", 0, "w_in", 0, qa, 2 * kva, kt, "x", 0)
    for n in range(qa // COLS):
        job("qk", n, "w_in", 0, n * COLS, COLS, kt, "x", 0)
    for n in range(2 * qb // COLS):
        job("qk", n + qa // COLS, "w_in", 0, b0 + n * COLS, COLS, kt, "x", 0)
    for n in range(qb // COLS):
        job("v", n, "w_in", 0, b0 + 2 * qb + n * COLS, COLS, kt, "x", 0)
    for n in range(d // COLS):
        job("ga", n, "w_in", 0, ga0 + n * COLS, COLS, kt, "x", 0)
    loops = []
    start = len(jobs)
    for n in range(d // COLS):
        job("gb", n, "w_in", 0, ga0 + d + n * COLS, COLS, kt, "x", 0, 0)
        job("ba", n, "w_branch_a", 0, n * COLS, COLS, kb, "o", 0, 1)
        job("bb", n, "w_branch_b", 0, n * COLS, COLS, kb, "o", kb, 2)
    loops.append((start + 3, 3, d // COLS - 1))
    turn[0] = 0
    for n in range(d // COLS):
        job("out", n, "w_out", 0, n * COLS, COLS, kt, "m", 0)
    blocks = dff // COLS
    down = 0
    for ff in range(0, blocks, FF_BLOCKS):
        k = min(FF_BLOCKS, blocks - ff)
        start = len(jobs)
        for n in range(k):
            job("gate", ff + n, "w_ffn_gate", 0, (ff + n) * COLS, COLS, kt, "h", 0)
            job("up", ff + n, "w_ffn_up", 0, (ff + n) * COLS, COLS, kt, "h", 0).slot = n
        loops.append((start + 2, 2, k - 1))
        for n in range(d // COLS):
            job("down", n, "w_ffn_down", ff * COLS, n * COLS, COLS, k * GROUP, "f", 0).done = down
            down += 1
    last_of, piece, sets = {}, 0, 0
    for a, j in enumerate(jobs):
        j.piece0 = piece
        piece += j.pieces
        j.prev = jobs[a - 1] if a else None
        j.before = last_of.get(j.pair)
        last_of[j.pair] = j
        if j.kind in ("qk", "kv", "bb", "out", "up"):
            j.set = sets
            sets += 1
    at = 0
    for start, width, count in loops:
        segments.append(jobs[at:start])
        segments.append((jobs[start:start + width], jobs[start + width:start + 2 * width], count))
        at = start + width * count
    segments.append(jobs[at:])
    return jobs, segments


def build(nc, x, norm_mix_g, w_in, q_norm_a, k_norm_a, sink_a, t5_bias, q_norm_b, k_norm_b, rel_bias_b,
          w_branch_a, w_branch_b, w_out, norm_ffn_g, w_ffn_gate, w_ffn_up, w_ffn_down, onehot, out):
    _, S, D = x.shape
    T = S // P
    KT = D // P
    NB = D // COLS
    QA, QB = w_branch_a.shape[1], w_branch_b.shape[1]
    KVA = (w_in.shape[2] - QA - 3 * QB - 2 * D) // 2
    HA = QA // HD
    KVH = KVA // HD
    PAIRS = QA // P
    NATT = 2 * PAIRS
    NH = COLS // HD
    NG = 2 * KT + 4
    HP = P // 2
    assert T == 2 and KVA == P and QA == QB and HA == t5_bias.shape[1] and S == 4 * HD
    jobs, segments = plan(D, QA, KVA, QB, w_ffn_gate.shape[2])
    weights = {"w_in": w_in, "w_branch_a": w_branch_a, "w_branch_b": w_branch_b, "w_out": w_out,
               "w_ffn_gate": w_ffn_gate, "w_ffn_up": w_ffn_up, "w_ffn_down": w_ffn_down}
    ATT_PIECE0 = next(j.piece0 for j in jobs if j.kind == "ga")
    LAST_DOWN = jobs[-1].done

    with ExitStack() as ctx:
        top = [nc.sbuf_base + (-nc.sbuf_base) % 64]

        def take(nbytes):
            offset = top[0]
            top[0] += nbytes + (-nbytes) % 32
            return offset

        def at(name, shape, dt, offset):
            return nc.alloc_sbuf_tensor_at(name, shape, dt, offset=offset)

        def sb(name, shape, dt=F32):
            return at(name, shape, dt, take(int(np.prod(shape[1:])) * 4))

        def sem(name):
            return ctx.enter_context(nc.semaphore(name))

        raw = sb("raw", [P, RAW_SLOTS, CHUNK_KT * COLS])
        w_hi = sb("w_hi", [P, SPLIT_SLOTS, PIECE_KT * COLS], F32R)
        w_lo = sb("w_lo", [P, SPLIT_SLOTS, PIECE_KT * COLS], F32R)
        xT_hi = sb("xT_hi", [P, KT, S], F32R)
        xT_lo = sb("xT_lo", [P, KT, S], F32R)
        o_oT = top[0]
        oT_hi = sb("oT_hi", [P, KT, S], F32R)
        oT_lo = sb("oT_lo", [P, KT, S], F32R)
        squares = at("squares", [P, T, D], F32, o_oT)
        o_att = take(2 * KT * S * 4)
        qT = at("qT", [P, 3 * PAIRS, S], F32, o_att)
        kT_a = at("kT_a", [P, KVH, S], F32, o_att + 3 * PAIRS * S * 4)
        mT_hi = at("mT_hi", [P, KT, S], F32R, o_att)
        mT_lo = at("mT_lo", [P, KT, S], F32R, o_att + KT * S * 4)
        o_v = take(T * (QB + KVA) * 4)
        v_b = at("v_b", [P, T, QB], F32, o_v)
        v_a = at("v_a", [P, T, KVA], F32, o_v + T * QB * 4)
        t5_hot = at("t5_hot", [t5_bias.shape[0], REL], F32, o_v)
        table_sb = at("table_sb", [HA, REL], F32, o_v + REL * 4)
        g_rows = at("g_rows", [NG - KT, P], F32, o_v + 2 * REL * 4)
        bias = sb("bias", [P, BIAS_SLOTS, 2, 2 * P])
        h = at("h", [P, T, D], F32, o_v)
        o_gate = take(T * D * 4)
        x_rows = at("x_rows", [P, T, D], F32, o_gate)
        gate_a = at("gate_a", [P, T, D], F32, o_gate)
        o_stage = take(4 * 2 * 3 * P * 4)
        prob = at("prob", [P, 2, 2, 3 * P], F32, o_stage)
        probT = at("probT", [P, 2, 2, 3 * P], F32, o_stage + 2 * 2 * 3 * P * 4)
        side_a = at("side_a", [P, T, COLS], F32, o_stage)
        side_b = at("side_b", [P, T, COLS], F32, o_stage + T * COLS * 4)
        staged = at("staged", [P, T, COLS], F32, o_stage + 2 * T * COLS * 4)
        ident = sb("ident", [P, P])
        mix_rows = sb("mix_rows", [KT, P])
        g_col = sb("g_col", [P, NG])
        gq = sb("gq", [P, 2])
        sink = sb("sink", [P, HA])
        t5 = sb("t5", [t5_bias.shape[0], HA])
        minus_half = sb("minus_half", [P, T * NH])
        x_ss = sb("x_ss", [P, T])
        x_ms = sb("x_ms", [P, T])
        x_rs = sb("x_rs", [P, T])
        h_ss = sb("h_ss", [P, T, NB])
        h_sum = sb("h_sum", [P, T])
        h_ms = sb("h_ms", [P, T])
        h_rs = sb("h_rs", [P, T])
        q_ss = sb("q_ss", [P, T * NH])
        q_ms = sb("q_ms", [P, T * NH])
        q_rs = sb("q_rs", [P, T * NH])
        top_logit = sb("top_logit", [P, 2, 4])
        minus_top = sb("minus_top", [P, 2, 4])
        row_sum = sb("row_sum", [P, 2, 4])
        sink_gap = sb("sink_gap", [P, 2, 4])
        sink_exp = sb("sink_exp", [P, 2, 4])
        denom = sb("denom", [P, 2, 4])
        inv = sb("inv", [P, 2, 4])
        assert top[0] <= nc.sbuf_usable_end
        table = nc.dram_tensor("bias_table_a", [HA, REL], F32, kind="Internal").ap()

        bank = [ctx.enter_context(nc.psum_tensor(f"bank{i}", [P, COLS], F32)) for i in range(8)]
        S_BANK, T_BANK = 4, 6

        first_landed = sem("first_landed")
        landed = [sem(f"landed{i}") for i in range(RAW_SLOTS)]
        hi_ready = sem("hi_ready")
        lo_ready = sem("lo_ready")
        piece_used = sem("piece_used")
        x_landed = [sem(f"x_landed{i}") for i in range(NB)]
        mix_landed = sem("mix_landed")
        g_landed = sem("g_landed")
        sink_landed = sem("sink_landed")
        t5_landed = sem("t5_landed")
        table_stored = sem("table_stored")
        bias_landed = [sem(f"bias_landed{i}") for i in range(BIAS_SLOTS)]
        h_landed = sem("h_landed")
        out_stored = sem("out_stored")
        ident_ready = sem("ident_ready")
        masks_ready = sem("masks_ready")
        g_turned = sem("g_turned")
        g_ready = sem("g_ready")
        table_made = sem("table_made")
        table_copied = sem("table_copied")
        pool_step = sem("pool_step")
        dve_step = sem("dve_step")
        x_ss_ready = sem("x_ss_ready")
        x_rs_ready = sem("x_rs_ready")
        h_ss_ready = sem("h_ss_ready")
        h_sum_ready = sem("h_sum_ready")
        h_rs_ready = sem("h_rs_ready")
        x_turned = sem("x_turned")
        scaled_ready = sem("scaled_ready")
        scaled_hi = sem("scaled_hi")
        xT_ready = sem("xT_ready")
        heads_ready = sem("heads_ready")
        q_ss_ready = sem("q_ss_ready")
        q_rs_ready = sem("q_rs_ready")
        heads_normed = sem("heads_normed")
        turned = sem("turned")
        qk_ready = sem("qk_ready")
        v_ready = sem("v_ready")
        scores_ready = sem("scores_ready")
        scores_read = sem("scores_read")
        top_ready = sem("top_ready")
        exp_ready = sem("exp_ready")
        prob_ready = sem("prob_ready")
        prob_turned = sem("prob_turned")
        probT_ready0 = sem("probT_ready0")
        probT_ready1 = sem("probT_ready1")
        o_summed = sem("o_summed")
        o_hi = sem("o_hi")
        o_ready = sem("o_ready")
        ga_ready = sem("ga_ready")
        ga_open = sem("ga_open")
        gb_open = sem("gb_open")
        branch_a_gated = sem("branch_a_gated")
        branch_b_gated = sem("branch_b_gated")
        merged = sem("merged")
        rows_hi = sem("rows_hi")
        mT_ready = sem("mT_ready")
        fT_ready = sem("fT_ready")
        h_ready = sem("h_ready")
        gate_open = sem("gate_open")
        gate_ready = sem("gate_ready")
        hidden_ready = sem("hidden_ready")
        h_added = sem("h_added")

        lhs = {"x": (xT_hi, xT_lo), "o": (oT_hi, oT_lo), "m": (mT_hi, mT_lo), "h": (xT_hi, xT_lo),
               "f": (oT_hi, oT_lo)}

        def evacuated(j):
            return {"qk": lambda: (heads_ready, j.set + 1), "kv": lambda: (heads_ready, j.set + 1),
                    "v": lambda: (v_ready, j.n + 1), "ga": lambda: (ga_ready, j.n + 1),
                    "gb": lambda: (gb_open, T * (j.n + 1)), "ba": lambda: (branch_a_gated, T * (j.n + 1)),
                    "bb": lambda: (branch_b_gated, T * (j.n + 1)), "out": lambda: (h_ready, j.n + 1),
                    "gate": lambda: (gate_ready, T * (j.n + 1)), "up": lambda: (hidden_ready, j.n + 1),
                    "down": lambda: (h_added, j.done + 1)}[j.kind]()

        def staged_for(j):
            return {"qk": lambda: (heads_normed, j.set + 1), "kv": lambda: (heads_normed, j.set + 1),
                    "bb": lambda: (merged, j.n + 1), "out": lambda: (h_ready, j.n + 1),
                    "up": lambda: (hidden_ready, j.n + 1)}[j.kind]()

        def set_read(j):
            return {"qk": lambda: (qk_ready, T * (j.set + 1)), "kv": lambda: (qk_ready, T * (j.set + 1)),
                    "bb": lambda: (mT_ready, T * (j.n + 1)), "out": lambda: (scaled_ready, NB + j.n + 1),
                    "up": lambda: (fT_ready, T * (j.n + 1))}[j.kind]()

        def columns(j):
            return bass.ds(j.n * COLS, COLS) if not isinstance(j.n, int) else slice(j.n * COLS, (j.n + 1) * COLS)

        def groups(n):
            return bass.ds(n * GROUP, GROUP) if not isinstance(n, int) else slice(n * GROUP, (n + 1) * GROUP)

        def tokens(t):
            return slice(t * P, (t + 1) * P)

        def scores_of(tile, e, t):
            return tile[:, e, 0:2 * P] if t else tile[:, e, 2 * P:3 * P]

        def att_step(j, k, ahead):
            a = j.piece0 + k - ATT_PIECE0 - ahead
            return a if a >= 0 and isinstance(j.off, int) else -1

        def run(engine, do_job):
            for segment in segments:
                if isinstance(segment, list):
                    for j in segment:
                        do_job(j)
                else:
                    first, second, count = segment
                    with engine.Fori(0, count) as i:
                        for a, b in zip(first, second):
                            do_job(stepped(a, b, i))

        block = ctx.enter_context(nc.Block())

        @block.sync
        def _(sp):
            x_view = x[0].rearrange("(t p) d -> p t d", p=P)
            out_view = out[0].rearrange("(t p) d -> p t d", p=P)

            def load_chunk(j, q):
                c = j.piece0 // 2 + q
                slot = c % RAW_SLOTS
                if c >= RAW_SLOTS:
                    sp.wait_ge(lo_ready, 2 * (c - RAW_SLOTS) + 2 + j.off)
                w = weights[j.weight]
                rows = slice(j.row0 + q * CHUNK_KT * P, j.row0 + (q + 1) * CHUNK_KT * P)
                src = w[0, rows, bass.ds(j.col0, j.cols)].rearrange("(k p) n -> p k n", p=P)
                dst = raw[:, slot, 0:CHUNK_KT * j.cols].rearrange("p (k n) -> p k n", n=j.cols)
                if c == 0:
                    sp.dma_start(dst[:, 0:PIECE_KT, :], src[:, 0:PIECE_KT, :]).then_inc(first_landed, 16)
                    dst, src = dst[:, PIECE_KT:, :], src[:, PIECE_KT:, :]
                sp.dma_start(dst, src).then_inc(landed[slot], 16)

            def load_bias(i):
                b, n = i % 2, i // 2
                slot = i % BIAS_SLOTS
                if i >= BIAS_SLOTS:
                    sp.wait_ge(scores_read, i - BIAS_SLOTS + 1)
                if b:
                    src, pitch, origin = rel_bias_b, rel_bias_b.shape[2], (rel_bias_b.shape[2] - 1) // 2 - ORIGIN
                    parts = ((0, 0, 4 * HD), (HP, 0, 3 * HD))
                else:
                    src, pitch, origin = table, REL, 0
                    parts = ((0, 2 * HD, 2 * HD), (HP, HD, 2 * HD))
                for p0, key0, keys in parts:
                    rows = bass.AP(src.tensor, src.offset + 2 * n * pitch + origin + p0 + key0,
                                   [[1, HP], [pitch, 2], [1, keys]])
                    sp.dma_start(bias[p0:p0 + HP, slot, :, key0:key0 + keys], rows).then_inc(bias_landed[slot], 16)

            def do_job(j):
                for q in range(j.pieces // 2):
                    if j.prev is None:
                        cs = slice(q * COLS, (q + 1) * COLS)
                        sp.dma_start(x_rows[:, :, cs], x_view[:, :, cs]).then_inc(x_landed[q], 16)
                    load_chunk(j, q)
                    i = att_step(j, 2 * q, 6)
                    if i >= 0 and i // 2 < NATT:
                        if i == 0:
                            sp.wait_ge(table_stored, 16)
                            sp.wait_ge(masks_ready, 1)
                        load_bias(i // 2)
                if j.kind == "bb" and j.first:
                    sp.wait_ge(o_ready, NATT)
                    sp.dma_start(h[:], x_view).then_inc(h_landed, 16)

            sp.dma_start(mix_rows[:], norm_mix_g[0].rearrange("(k p) -> k p", p=P)).then_inc(mix_landed, 16)
            run(sp, do_job)
            for n in range(NB):
                cs = slice(n * COLS, (n + 1) * COLS)
                sp.wait_ge(h_added, LAST_DOWN - NB + n + 2)
                sp.dma_start(out_view[:, :, cs], h[:, :, cs]).then_inc(out_stored, 16)
            sp.wait_ge(out_stored, 16 * NB)

        @block.gpsimd
        def _(pool):
            steps = [0]

            def in_order(ins):
                steps[0] += 1
                ins.then_inc(pool_step, 1)
                pool.wait_ge(pool_step, steps[0])

            in_order(nc.gpsimd.memset(ident[:], 0.0))
            nc.gpsimd.affine_select(out=ident[:], in_=ident[:], compare_op=ALU.not_equal, fill=1.0, base=0,
                                    pattern=[[-1, P]], channel_multiplier=1).then_inc(ident_ready, 1)
            in_order(nc.gpsimd.memset(minus_half[:], -0.5))
            pool.dma_start(g_rows[0:KT, :], norm_ffn_g[0].rearrange("(k p) -> k p", p=P)).then_inc(g_landed, 16)
            for r, g in enumerate((q_norm_a, k_norm_a, q_norm_b, k_norm_b)):
                pool.dma_start(g_rows[KT + r:KT + r + 1, :],
                              bass.AP(g.tensor, g.offset, [[HD, 1], [0, 2], [1, HD]])).then_inc(g_landed, 16)
            pool.dma_start(sink[:], bass.AP(sink_a.tensor, sink_a.offset, [[0, P], [1, HA]])).then_inc(sink_landed, 16)
            pool.dma_start(t5[:], t5_bias).then_inc(t5_landed, 16)
            pool.dma_start(t5_hot[:], onehot).then_inc(t5_landed, 16)

            def rsqrt(dst, mean, sums, n, width, ready):
                in_order(nc.gpsimd.tensor_scalar(mean, sums, 1.0 / n, EPS, ALU.mult, ALU.add))
                nc.gpsimd.tensor_tensor(dst, mean, minus_half[:, 0:width], ALU.pow).then_inc(ready, 1)

            pool.wait_ge(x_ss_ready, T)
            rsqrt(x_rs[:], x_ms[:], x_ss[:], D, T, x_rs_ready)
            pool.wait_ge(table_copied, 1)
            pool.dma_start(table, table_sb[:]).then_inc(table_stored, 16)
            for j in (j for j in jobs if j.kind in ("qk", "kv")):
                width = T * (j.cols if j.kind == "qk" else KVA) // HD
                pool.wait_ge(q_ss_ready, j.set + 1)
                if j.set:
                    pool.wait_ge(heads_normed, j.set)
                rsqrt(q_rs[:, 0:width], q_ms[:, 0:width], q_ss[:, 0:width], HD, width, q_rs_ready)
            pool.wait_ge(h_sum_ready, 1)
            rsqrt(h_rs[:], h_ms[:], h_sum[:], D, T, h_rs_ready)

        @block.scalar
        def _(act):
            A = nc.scalar.activation

            def split_hi(j, k):
                p = j.piece0 + k
                c = p // 2
                if p == 0:
                    act.wait_ge(first_landed, 16)
                else:
                    act.wait_ge(landed[c % RAW_SLOTS], 16 * (c // RAW_SLOTS + 1) + 2 * j.off)
                if p >= SPLIT_SLOTS:
                    act.wait_ge(piece_used, p - SPLIT_SLOTS + 1 + j.off)
                w = PIECE_KT * j.cols
                A(w_hi[:, p % SPLIT_SLOTS, 0:w], raw[:, c % RAW_SLOTS, (p % 2) * w:(p % 2 + 1) * w],
                  ACT.Copy).then_inc(hi_ready, 1)

            def out_of_psum(j, dst, cols, func=ACT.Copy, scale=x_rs):
                for t in range(T):
                    ins = A(dst(t), bank[2 * j.pair + t][:, cols], func, scale=scale[:, t:t + 1])
                return ins

            def scaled_to_hi(n, at_group):
                act.wait_ge(scaled_ready, n + 1)
                A(xT_hi[:, groups(at_group), :].rearrange("p k (t s) -> p t k s", t=T),
                  staged[:].rearrange("p t (k s) -> p t k s", k=GROUP), ACT.Copy).then_inc(scaled_hi, 1)

            def turned_to_hi(j, dst, at_group):
                act.wait_ge(turned, j.set + 1)
                for t in range(T):
                    A(dst[:, groups(at_group), tokens(t)], bank[T_BANK + t][:].rearrange("p (k s) -> p k s", k=GROUP),
                      ACT.Copy).then_inc(rows_hi, 1)

            def turned_to_heads(j):
                act.wait_ge(turned, j.set + 1)
                if j.first:
                    act.wait_ge(g_ready, 4)
                for t in range(T):
                    if j.kind == "kv":
                        dst, kvs = kT_a[:, :, tokens(t)], KVH
                        scale = g_col[:, 2 * KT + 1:2 * KT + 2]
                    else:
                        dst, kvs = qT[:, groups(j.n), tokens(t)], GROUP
                        if j.n < (QA + QB) // COLS:
                            dst = dst[:, :, ::-1]
                            b = j.n // (QA // COLS)
                            scale = gq[:, b:b + 1]
                        else:
                            scale = g_col[:, 2 * KT + 3:2 * KT + 4]
                    A(dst, bank[T_BANK + t][:, 0:kvs * P].rearrange("p (k s) -> p k s", k=kvs), ACT.Copy,
                      scale=scale).then_inc(qk_ready, 1)

            def follow(j, k):
                if k == 3 and j.kind in ("qk", "kv", "v", "ga", "gb", "gate"):
                    act.wait_ge(piece_used, j.piece0 + j.pieces + j.off)
                if j.kind in ("qk", "kv") and k == 3:
                    if j.set == 0:
                        act.wait_ge(x_rs_ready, 1)
                    else:
                        act.wait_ge(heads_normed, j.set)
                    if j.kind == "qk":
                        out_of_psum(j, lambda t: side_a[:, t, :], slice(0, COLS)).then_inc(heads_ready, 1)
                    else:
                        out_of_psum(j, lambda t: v_a[:, t, :], slice(KVA, 2 * KVA))
                        out_of_psum(j, lambda t: side_a[:, t, 0:KVA], slice(0, KVA)).then_inc(heads_ready, 1)
                if j.kind in ("qk", "kv") and k == 7:
                    turned_to_heads(j)
                if j.kind == "v" and k == 3:
                    act.wait_ge(table_stored, 16)
                    out_of_psum(j, lambda t: v_b[:, t, columns(j)], slice(0, COLS)).then_inc(v_ready, 1)
                if j.kind == "ga" and k == 3:
                    act.wait_ge(x_turned, NB)
                    out_of_psum(j, lambda t: gate_a[:, t, columns(j)], slice(0, COLS)).then_inc(ga_ready, 1)
                if j.kind == "gb" and k == 3:
                    act.wait_ge(ga_ready, NB)
                    if not j.first:
                        act.wait_ge(merged, j.n)
                    for t in range(T):
                        A(gate_a[:, t, columns(j)], gate_a[:, t, columns(j)], ACT.Sigmoid).then_inc(ga_open, 1)
                        A(side_a[:, t, :], bank[2 * j.pair + t][:], ACT.Sigmoid,
                          scale=x_rs[:, t:t + 1]).then_inc(gb_open, 1)
                if j.kind == "bb" and k == 5:
                    turned_to_hi(j, mT_hi, j.n)
                if j.kind == "out" and k == 4:
                    act.wait_ge(h_ready, j.n + 1)
                    if j.n:
                        act.wait_ge(h_ss_ready, T * j.n)
                    for t in range(T):
                        A(side_b[:, t, :], h[:, t, columns(j)], ACT.Square,
                          accum_out=h_ss[:, t, j.n:j.n + 1]).then_inc(h_ss_ready, 1)
                if j.kind == "out" and k == 6:
                    scaled_to_hi(NB + j.n, j.n)
                if j.kind == "gate" and k == 3:
                    if j.first:
                        act.wait_ge(h_rs_ready, 1)
                    else:
                        act.wait_ge(gate_ready, T * j.n)
                    for t in range(T):
                        A(side_a[:, t, :], bank[2 * j.pair + t][:], ACT.Sigmoid,
                          scale=h_rs[:, t:t + 1]).then_inc(gate_open, 1)
                if j.kind == "up" and k == 5:
                    turned_to_hi(j, oT_hi, j.slot)

            def exp_scores(i):
                s = i % 2
                act.wait_ge(top_ready, i + 1)
                for e in range(2):
                    for t in range(T):
                        v = scores_of(prob[:, s], e, t)
                        q = 2 * e + t
                        A(v, v, ACT.Exp, bias=minus_top[:, s, q:q + 1],
                          accum_out=row_sum[:, s, q:q + 1]).then_inc(exp_ready, 1)
                A(sink_exp[:, s, :], sink_gap[:, s, :], ACT.Exp).then_inc(exp_ready, 1)

            def copy_probT(i):
                act.wait_ge(prob_turned, i + 1)
                A(probT[:, i % 2, 0, :], bank[T_BANK][:, 0:3 * P], ACT.Copy).then_inc(probT_ready0, 1)

            def split_o(i):
                act.wait_ge(o_summed, i + 1)
                A(oT_hi[:, (i % 2) * PAIRS + i // 2, :], bank[T_BANK][:, 0:S], ACT.Copy).then_inc(o_hi, 1)

            act.wait_ge(ident_ready, 1)
            A(sink_gap[:, 0, :], ident[:, 0:4], ACT.Copy)

            def do_job(j):
                for k in range(j.pieces):
                    if j.prev is None and k % 2 == 0:
                        scaled_to_hi(k // 2, k // 2)
                    split_hi(j, k)
                    if j.prev is None and k in (5, 7):
                        for q in range(NB):
                            act.wait_ge(x_landed[q], 16)
                        t = (k - 5) // 2
                        A(squares[:, t, :], x_rows[:, t, :], ACT.Square,
                          accum_out=x_ss[:, t:t + 1]).then_inc(x_ss_ready, 1)
                    if j.prev is not None:
                        follow(j.prev, k)
                    a = att_step(j, k, SPLIT_SLOTS)
                    if a >= 0:
                        if a % 2 == 0 and a // 2 < NATT:
                            exp_scores(a // 2)
                        if 1 <= a // 2 <= NATT:
                            (split_o if a % 2 else copy_probT)(a // 2 - 1)

            run(act, do_job)

        @block.vector
        def _(dve):
            V = nc.vector
            steps = [0]

            def in_order(ins):
                steps[0] += 1
                ins.then_inc(dve_step, 1)
                dve.wait_ge(dve_step, steps[0])

            def split_lo(j, k):
                p = j.piece0 + k
                dve.wait_ge(hi_ready, p + 1 + j.off)
                w = PIECE_KT * j.cols
                V.tensor_tensor(w_lo[:, p % SPLIT_SLOTS, 0:w],
                                raw[:, p // 2 % RAW_SLOTS, (p % 2) * w:(p % 2 + 1) * w],
                                w_hi[:, p % SPLIT_SLOTS, 0:w].bitcast(F32), ALU.subtract).then_inc(lo_ready, 1)

            def scale_rows(first_bank, g0, n):
                if n:
                    dve.wait_ge(xT_ready, n)
                for t in range(T):
                    ins = V.tensor_tensor(staged[:, t, :].rearrange("p (k s) -> p k s", k=GROUP),
                                          bank[first_bank + t][:].rearrange("p (k s) -> p k s", k=GROUP),
                                          g_col[:, g0:g0 + GROUP, None].to_broadcast([P, GROUP, P]), ALU.mult)
                ins.then_inc(scaled_ready, 1)

            def scaled_to_lo(n, at_group):
                dve.wait_ge(scaled_hi, n + 1)
                turn = "p k (t s) -> p t k s"
                V.tensor_tensor(xT_lo[:, groups(at_group), :].rearrange(turn, t=T),
                                staged[:].rearrange("p t (k s) -> p t k s", k=GROUP),
                                xT_hi[:, groups(at_group), :].bitcast(F32).rearrange(turn, t=T),
                                ALU.subtract).then_inc(xT_ready, 1)

            def turned_to_lo(dst_hi, dst_lo, at_group, sets_before, ready):
                for t in range(T):
                    dve.wait_ge(rows_hi, T * sets_before + t + 1)
                    V.tensor_tensor(dst_lo[:, groups(at_group), tokens(t)],
                                    bank[T_BANK + t][:].rearrange("p (k s) -> p k s", k=GROUP),
                                    dst_hi[:, groups(at_group), tokens(t)].bitcast(F32),
                                    ALU.subtract).then_inc(ready, 1)

            def head_view(tile, nh):
                return tile[:, :, 0:nh * HD].rearrange("p t (h d) -> p t h d", d=HD)

            def add_to_h(j, ready):
                for t in range(T):
                    ins = V.tensor_tensor(h[:, t, columns(j)], bank[2 * j.pair + t][:], h[:, t, columns(j)], ALU.add)
                ins.then_inc(ready, 1)

            def follow(j, k):
                if k == 3 and j.kind in ("ba", "bb", "out", "up", "down"):
                    dve.wait_ge(piece_used, j.piece0 + j.pieces + j.off)
                if j.kind in ("qk", "kv"):
                    nh = NH if j.kind == "qk" else KVH
                    heads = head_view(side_a, nh)
                    if k == 3:
                        dve.wait_ge(heads_ready, j.set + 1)
                        in_order(V.tensor_tensor(head_view(side_b, nh), heads, heads, ALU.mult))
                        if j.set:
                            dve.wait_ge(q_rs_ready, j.set)
                        V.tensor_reduce(q_ss[:, 0:T * nh], head_view(side_b, nh), AX.X, ALU.add)\
                            .then_inc(q_ss_ready, 1)
                    if k == 4:
                        dve.wait_ge(q_rs_ready, j.set + 1)
                        if j.set:
                            dve.wait_ge(turned, j.set)
                        rs = q_rs[:, 0:T * nh].rearrange("p (t h) -> p t h", t=T)[:, :, :, None]\
                            .to_broadcast([P, T, nh, HD])
                        if j.kind == "qk":
                            V.tensor_tensor(head_view(staged, nh), heads, rs, ALU.mult).then_inc(heads_normed, 1)
                        else:
                            twice = staged[:, :, 0:2 * nh * HD].rearrange("p t (h c d) -> p t h c d", h=nh, c=2)
                            V.tensor_tensor(twice[:, :, :, 0, :], heads, rs, ALU.mult)
                            V.tensor_tensor(twice[:, :, :, 1, :], heads, rs, ALU.mult).then_inc(heads_normed, 1)
                if j.kind == "ba" and k == 3:
                    if not j.first:
                        dve.wait_ge(merged, j.n)
                    for t in range(T):
                        dve.wait_ge(ga_open, T * j.n + t + 1)
                        V.tensor_tensor(side_b[:, t, :], bank[2 * j.pair + t][:], gate_a[:, t, columns(j)],
                                        ALU.mult).then_inc(branch_a_gated, 1)
                if j.kind == "bb" and k == 3:
                    for t in range(T):
                        dve.wait_ge(gb_open, T * j.n + t + 1)
                        V.tensor_tensor(side_a[:, t, :], bank[2 * j.pair + t][:], side_a[:, t, :],
                                        ALU.mult).then_inc(branch_b_gated, 1)
                    dve.wait_ge(branch_b_gated, T * (j.n + 1))
                    dve.wait_ge(turned, j.set)
                    V.tensor_tensor(staged[:], side_a[:], side_b[:], ALU.add).then_inc(merged, 1)
                if j.kind == "bb" and k == 5:
                    turned_to_lo(mT_hi, mT_lo, j.n, j.n, mT_ready)
                if j.kind == "out":
                    if k == 3:
                        dve.wait_ge(h_landed, 16)
                        add_to_h(j, h_ready)
                    if k == 5:
                        dve.wait_ge(turned, j.set + 1)
                        scale_rows(T_BANK, KT + j.n * GROUP, NB + j.n)
                        if j.n == NB - 1:
                            dve.wait_ge(h_ss_ready, T * NB)
                            V.tensor_reduce(h_sum[:], h_ss[:], AX.X, ALU.add).then_inc(h_sum_ready, 1)
                    if k == 6:
                        scaled_to_lo(NB + j.n, j.n)
                if j.kind == "gate" and k == 3:
                    for t in range(T):
                        dve.wait_ge(gate_open, T * j.n + t + 1)
                        V.scalar_tensor_tensor(side_b[:, t, :], bank[2 * j.pair + t][:], h_rs[:, t:t + 1],
                                               side_a[:, t, :], ALU.mult, ALU.mult).then_inc(gate_ready, 1)
                if j.kind == "up" and k == 3:
                    dve.wait_ge(gate_ready, T * (j.n + 1))
                    dve.wait_ge(turned, j.set)
                    for t in range(T):
                        ins = V.scalar_tensor_tensor(staged[:, t, :], bank[2 * j.pair + t][:], h_rs[:, t:t + 1],
                                                     side_b[:, t, :], ALU.mult, ALU.mult)
                    ins.then_inc(hidden_ready, 1)
                if j.kind == "up" and k == 5:
                    turned_to_lo(oT_hi, oT_lo, j.slot, NB + j.n, fT_ready)
                if j.kind == "down" and k == 3:
                    add_to_h(j, h_added)

            def softmax_top(i):
                b, n, s = i % 2, i // 2, i % 2
                dve.wait_ge(scores_ready, i + 1)
                dve.wait_ge(bias_landed[i % BIAS_SLOTS], 2 * 16 * (i // BIAS_SLOTS + 1))
                if i == 0:
                    dve.wait_ge(sink_landed, 16)
                if i >= 2:
                    dve.wait_ge(prob_turned, i - 1)
                for e in range(2):
                    for t in range(T):
                        q = 2 * e + t
                        tile = bias[:, i % BIAS_SLOTS, e, :] if t else bias[:, i % BIAS_SLOTS, e, P:2 * P]
                        start = NEG if b else sink[:, 2 * n + e:2 * n + e + 1]
                        scores = bank[S_BANK + e][:, 0:2 * P] if t else bank[S_BANK + e][:, 2 * P:3 * P]
                        ins = V.tensor_tensor_reduce(out=scores_of(prob[:, s], e, t), in0=scores, in1=tile, scale=1.0,
                                                     scalar=start, op0=ALU.add, op1=ALU.max,
                                                     accum_out=top_logit[:, s, q:q + 1])
                ins.then_inc(scores_read, 1)
                dve.wait_ge(scores_read, i + 1)
                if b:
                    V.memset(sink_gap[:, s, :], NEG)
                else:
                    V.tensor_tensor(sink_gap[:, s, :].rearrange("p (e t) -> p e t", t=T),
                                    sink[:, 2 * n:2 * n + 2, None].to_broadcast([P, 2, T]),
                                    top_logit[:, s, :].rearrange("p (e t) -> p e t", t=T), ALU.subtract)
                V.tensor_scalar(minus_top[:, s, :], top_logit[:, s, :], -1.0, None, ALU.mult).then_inc(top_ready, 1)

            def softmax_scale(i):
                s = i % 2
                dve.wait_ge(exp_ready, 5 * (i + 1))
                in_order(V.tensor_tensor(denom[:, s, :], row_sum[:, s, :], sink_exp[:, s, :], ALU.add))
                in_order(V.reciprocal(inv[:, s, :], denom[:, s, :]))
                for e in range(2):
                    for t in range(T):
                        v = scores_of(prob[:, s], e, t)
                        V.tensor_scalar(v, v, inv[:, s, 2 * e + t:2 * e + t + 1], None, ALU.mult)\
                            .then_inc(prob_ready, 1)

            def copy_probT(i):
                dve.wait_ge(prob_turned, i + 1)
                V.tensor_copy(probT[:, i % 2, 1, :], bank[T_BANK + 1][:, 0:3 * P]).then_inc(probT_ready1, 1)

            def split_o(i):
                dve.wait_ge(o_hi, i + 1)
                at_kt = (i % 2) * PAIRS + i // 2
                V.tensor_tensor(oT_lo[:, at_kt, :], bank[T_BANK][:, 0:S], oT_hi[:, at_kt, :].bitcast(F32),
                                ALU.subtract).then_inc(o_ready, 1)

            for slot in range(BIAS_SLOTS):
                if slot % 2 == 0:
                    V.memset(bias[0:HP, slot, :, 0:2 * HD], NEG)
                    V.memset(bias[HP:P, slot, :, 0:HD], NEG)
                ins = V.memset(bias[HP:P, slot, :, 3 * HD:], NEG)
            ins.then_inc(masks_ready, 1)
            dve.wait_ge(g_turned, 1)
            V.tensor_copy(g_col[:, 0:KT], bank[0][:, 0:KT]).then_inc(g_ready, 1)
            dve.wait_ge(g_ready, 1)

            def do_job(j):
                for k in range(j.pieces):
                    if j.prev is None and k % 2 == 0:
                        g = k // 2
                        dve.wait_ge(x_turned, g + 1)
                        scale_rows(4 + 2 * (g % 2), g * GROUP, g)
                        scaled_to_lo(g, g)
                    split_lo(j, k)
                    if j.prev is None and k == 6:
                        dve.wait_ge(table_made, 1)
                        V.tensor_copy(g_col[:, KT:NG], bank[2][:, REL:REL + NG - KT]).then_inc(g_ready, 1)
                        V.tensor_copy(table_sb[:], bank[2][0:HA, 0:REL]).then_inc(table_copied, 1)
                        dve.wait_ge(g_ready, 2)
                        for b in range(2):
                            V.tensor_scalar(gq[:, b:b + 1], g_col[:, 2 * KT + 2 * b:2 * KT + 2 * b + 1],
                                            float(HD) ** -0.5, None, ALU.mult).then_inc(g_ready, 1)
                    if j.prev is not None:
                        follow(j.prev, k)
                    a = att_step(j, k, SPLIT_SLOTS - 1)
                    if a >= 0:
                        if a % 2 == 0:
                            if a // 2 < NATT:
                                softmax_top(a // 2)
                            if 2 <= a // 2 <= NATT + 1:
                                split_o(a // 2 - 2)
                        else:
                            if 1 <= a // 2 <= NATT:
                                copy_probT(a // 2 - 1)
                            if a // 2 < NATT:
                                softmax_scale(a // 2)

            run(dve, do_job)
            last = jobs[-1]
            dve.wait_ge(piece_used, last.piece0 + last.pieces)
            add_to_h(last, h_added)

        @block.tensor
        def _(pe):
            M = nc.tensor.matmul
            turn = nc.tensor.transpose

            def turn_x(g):
                pe.wait_ge(x_landed[g], 16)
                if g >= 2:
                    pe.wait_ge(scaled_ready, g - 1)
                for t in range(T):
                    for c in range(GROUP):
                        ins = turn(bank[4 + 2 * (g % 2) + t][:, c * P:(c + 1) * P],
                                   x_rows[:, t, g * COLS + c * P:g * COLS + (c + 1) * P], ident[:])
                ins.then_inc(x_turned, 1)

            def turn_set(j):
                pe.wait_ge(*staged_for(j))
                src = h[:, :, columns(j)] if j.kind == "out" else staged
                for t in range(T):
                    for g in range(KVH if j.kind == "kv" else GROUP):
                        ins = turn(bank[T_BANK + t][:, g * P:(g + 1) * P], src[:, t, g * P:(g + 1) * P], ident[:])
                ins.then_inc(turned, 1)

            def scores(i):
                b, n = i % 2, i // 2
                if i == 0:
                    pe.wait_ge(qk_ready, T * (3 * PAIRS // GROUP + 1))
                else:
                    pe.wait_ge(scores_read, i)
                for t in (1, 0):
                    for e in range(2):
                        rows = slice(e * HD, (e + 1) * HD)
                        keys = slice(0, (t + 1) * P)
                        k = qT[rows, 2 * PAIRS + n, keys] if b else kT_a[rows, 2 * n // (HA // KVH), keys]
                        dst = bank[S_BANK + e][:, 0:2 * P] if t else bank[S_BANK + e][:, 2 * P:3 * P]
                        ins = M(dst, qT[rows, b * PAIRS + n, tokens(t)], k, start=True, stop=True)
                ins.then_inc(scores_ready, 1)

            def turn_probs(i):
                pe.wait_ge(prob_ready, 4 * (i + 1))
                if i:
                    pe.wait_ge(o_ready, i)
                for e in range(2):
                    for c in range(3):
                        cs = slice(c * P, (c + 1) * P)
                        ins = turn(bank[T_BANK + e][:, cs], prob[:, i % 2, e, cs], ident[:])
                ins.then_inc(prob_turned, 1)

            def values(i):
                b, n = i % 2, i // 2
                pe.wait_ge(probT_ready0, i + 1)
                pe.wait_ge(probT_ready1, i + 1)
                if i == 0:
                    pe.wait_ge(v_ready, QB // COLS)
                for e in range(2):
                    rows = slice(e * HD, (e + 1) * HD)
                    v, col = (v_b, (2 * n + e) * HD) if b else (v_a, 2 * n // (HA // KVH) * HD)
                    keys0, keys1 = v[:, 0, col:col + HD], v[:, 1, col:col + HD]
                    part = [probT[:, i % 2, e, c * P:(c + 1) * P][:, ::-1] for c in range(3)]
                    M(bank[T_BANK][rows, 0:P], keys0, part[2], start=True, stop=True)
                    M(bank[T_BANK][rows, P:2 * P], keys0, part[0], start=True, stop=False)
                    ins = M(bank[T_BANK][rows, P:2 * P], keys1, part[1], start=False, stop=True)
                ins.then_inc(o_summed, 1)

            def operand_ready(j, kt):
                g = kt // GROUP
                if j.prev is None:
                    pe.wait_ge(xT_ready, g + 1)
                if j.kind == "ba" and j.first and g == 0:
                    pe.wait_ge(o_ready, NATT)
                if j.kind == "out" and j.first:
                    pe.wait_ge(mT_ready, T * (g + 1))
                if j.kind == "gate" and j.first:
                    pe.wait_ge(xT_ready, NB + g + 1)
                if j.kind == "down" and j.first:
                    pe.wait_ge(fT_ready, T * (j.row0 // COLS + g + 1))

            def multiply(j, k):
                p = j.piece0 + k
                hi, lo = lhs[j.lhs]
                pe.wait_ge(lo_ready, p + 1 + j.off)
                for q in range(PIECE_KT):
                    kt = k * PIECE_KT + q
                    if kt % GROUP == 0:
                        operand_ready(j, kt)
                    w = slice(q * j.cols, (q + 1) * j.cols)
                    for t in range(T):
                        sums = bank[2 * j.pair + t][:, 0:j.cols]
                        x_hi, x_lo = hi[:, j.kt0 + kt, tokens(t)], lo[:, j.kt0 + kt, tokens(t)]
                        M(sums, x_hi, w_hi[:, p % SPLIT_SLOTS, w], start=kt == 0, stop=False)
                        M(sums, x_lo, w_hi[:, p % SPLIT_SLOTS, w], start=False, stop=False)
                        ins = M(sums, x_hi, w_lo[:, p % SPLIT_SLOTS, w], start=False, stop=kt == j.kts - 1)
                ins.then_inc(piece_used, 1)

            pe.wait_ge(ident_ready, 1)
            turn_x(0)
            pe.wait_ge(mix_landed, 16)
            turn(bank[0][:, 0:KT], mix_rows[:], ident[0:KT, 0:KT]).then_inc(g_turned, 1)
            turn_x(1)
            pe.wait_ge(g_ready, 1)

            def do_job(j):
                if j.before is not None:
                    pe.wait_ge(*evacuated(j.before))
                elif j.pair == 1:
                    pe.wait_ge(table_copied, 1)
                for k in range(j.pieces):
                    a = att_step(j, k, 0)
                    if a >= 0 and a % 2 == 0 and a // 2 < NATT:
                        scores(a // 2)
                    multiply(j, k)
                    if j.prev is None and k in (0, 2):
                        turn_x(k // 2 + 2)
                    if j.prev is None and k == 5:
                        pe.wait_ge(g_landed, 16 * 5)
                        pe.wait_ge(t5_landed, 32)
                        turn(bank[2][:, REL:REL + NG - KT], g_rows[:], ident[0:NG - KT, 0:NG - KT])
                        M(bank[2][0:HA, 0:REL], t5[:], t5_hot[:], start=True, stop=True).then_inc(table_made, 1)
                    if j.prev is not None and j.prev.set is not None:
                        if k == (4 if j.prev.kind in ("qk", "kv") else 1):
                            turn_set(j.prev)
                        if k == j.pieces - 1:
                            pe.wait_ge(*set_read(j.prev))
                    if a >= 0 and 1 <= a // 2 <= NATT:
                        (values if a % 2 else turn_probs)(a // 2 - 1)

            run(pe, do_job)


_INS = ["x", "norm_mix_g", "w_in", "q_norm_a", "k_norm_a", "sink_a", "t5_bias", "q_norm_b", "k_norm_b", "rel_bias_b",
        "w_branch_a", "w_branch_b", "w_out", "norm_ffn_g", "w_ffn_gate", "w_ffn_up", "w_ffn_down"]


def t5_one_hot(buckets=32, max_dist=128):
    rel = np.arange(REL) - ORIGIN
    nb = buckets // 2
    exact = nb // 2
    n = np.abs(rel)
    large = exact + (np.log(np.maximum(n, 1) / exact) / np.log(max_dist / exact) * (nb - exact)).astype(np.int32)
    bucket = (rel > 0) * nb + np.where(n < exact, n, np.minimum(large, nb - 1))
    return (np.arange(buckets)[:, None] == bucket[None, :]).astype(np.float32)


def kernel(**inputs):
    import concourse.bacc as bacc
    from concourse.bass_utils import run_bass_kernel_spmd

    nc = bacc.Bacc("TRN2", target_bir_lowering=False, num_devices=1)
    arrays, args = {}, []
    for name in _INS + ["onehot"]:
        a = t5_one_hot() if name == "onehot" else np.ascontiguousarray(inputs[name])
        arrays[f"in_{name}"] = a
        args.append(nc.dram_tensor(f"in_{name}", a.shape, mybir.dt.from_np(a.dtype), kind="ExternalInput").ap())
    out = nc.dram_tensor("out", inputs["x"].shape, F32, kind="ExternalOutput").ap()
    build(nc, *args, out)
    r = run_bass_kernel_spmd(nc, [arrays], core_ids=[0])
    return r.results[0]["out"]
```
